# Optimizing a Trainium2 kernel written in Bass

```python
import math
import jax, jax.numpy as jnp
from jax import lax
import numpy as np

D_MODEL = 1024
BATCH = 1
SEQ = 512
DEPTH = 2

CHUNK = 64
Q_BLOCK = 128
EPS = 1e-6

MLA_HEADS = 6
MLA_Q_RANK = 256
MLA_KV_RANK = 128
MLA_NOPE = 64
MLA_ROPE = 32
MLA_V = 64
ROPE_THETA = 10000.0

DIFF_HEADS = 6
DIFF_QK = 32
DIFF_V = 2 * DIFF_QK

CH_HEADS = 4
CH_HD = 64
CH_LEFT = 8
CH_BAND = (CH_LEFT + 1) * CHUNK
REL_MAX = 256
N_REL = REL_MAX + CHUNK

MLA_WIDTH = MLA_HEADS * MLA_V
DIFF_WIDTH = DIFF_HEADS * DIFF_V
CH_WIDTH = CH_HEADS * CH_HD
MIX_WIDTH = MLA_WIDTH + DIFF_WIDTH + CH_WIDTH

IN_MLA = MLA_Q_RANK + MLA_KV_RANK + MLA_ROPE
IN_DIFF = 2 * DIFF_HEADS * 2 * DIFF_QK + DIFF_HEADS * DIFF_V
IN_CH = 3 * CH_WIDTH
IN_WIDTH = IN_MLA + IN_DIFF + IN_CH

D_FF = 2816
CONV_W = 3


def rms_norm(x, g):
    xf = x.astype(jnp.float32)
    y = xf * lax.rsqrt(jnp.mean(xf * xf, axis=-1, keepdims=True) + EPS)
    return (y * g.astype(jnp.float32)).astype(x.dtype)

def rope_cos_sin(pos, dim):
    half = dim // 2
    inv = ROPE_THETA ** (-jnp.arange(half, dtype=jnp.float32) / half)
    ang = pos.astype(jnp.float32)[..., None] * inv
    return jnp.cos(ang), jnp.sin(ang)

def apply_rope(x, cos, sin):
    half = x.shape[-1] // 2
    xf = x.astype(jnp.float32)
    x1, x2 = xf[..., :half], xf[..., half:]
    return jnp.concatenate([x1 * cos - x2 * sin, x1 * sin + x2 * cos], axis=-1).astype(x.dtype)

def alibi_slopes(n):
    return 2.0 ** (-8.0 * jnp.arange(1, n + 1, dtype=jnp.float32) / n)

def sweep_query_blocks(block_fn, seq):
    out = lax.map(block_fn, jnp.arange(seq // Q_BLOCK))
    out = jnp.moveaxis(out, 0, 1)
    return out.reshape(out.shape[0], seq, *out.shape[3:])

def chunk_causal_mask(start, seq):
    q_chunk = (start + jnp.arange(Q_BLOCK)) // CHUNK
    k_chunk = jnp.arange(seq) // CHUNK
    return k_chunk[None, :] <= q_chunk[:, None]

def mla_attention(h, pos, q_norm, w_uq, kv_norm, w_ukv):
    B, S, _ = h.shape
    c_q, c_kv, k_r = jnp.split(h, [MLA_Q_RANK, MLA_Q_RANK + MLA_KV_RANK], axis=-1)
    cos, sin = rope_cos_sin(pos, MLA_ROPE)
    q = (rms_norm(c_q, q_norm) @ w_uq).reshape(B, S, MLA_HEADS, MLA_NOPE + MLA_ROPE)
    q_nope = q[..., :MLA_NOPE]
    q_rope = apply_rope(q[..., MLA_NOPE:], cos[:, :, None, :], sin[:, :, None, :])
    kv = (rms_norm(c_kv, kv_norm) @ w_ukv).reshape(B, S, MLA_HEADS, MLA_NOPE + MLA_V)
    k_nope, v = kv[..., :MLA_NOPE], kv[..., MLA_NOPE:]
    k_rope = apply_rope(k_r, cos, sin)
    scale = (MLA_NOPE + MLA_ROPE) ** -0.5

    def block(i):
        start = i * Q_BLOCK
        qn = lax.dynamic_slice_in_dim(q_nope, start, Q_BLOCK, axis=1)
        qr = lax.dynamic_slice_in_dim(q_rope, start, Q_BLOCK, axis=1)
        s = (jnp.einsum('bqhd,bkhd->bhqk', qn, k_nope)
             + jnp.einsum('bqhr,bkr->bhqk', qr, k_rope)).astype(jnp.float32) * scale
        s = jnp.where(chunk_causal_mask(start, S), s, -jnp.inf)
        p = jax.nn.softmax(s, axis=-1)
        return jnp.einsum('bhqk,bkhd->bqhd', p.astype(v.dtype), v)

    return sweep_query_blocks(block, S).reshape(B, S, MLA_WIDTH)

def diff_attention(h, pos, lam, sub_norm, lam_init, slopes):
    B, S, _ = h.shape
    qk_w = DIFF_HEADS * 2 * DIFF_QK
    q, k, v = jnp.split(h, [qk_w, 2 * qk_w], axis=-1)
    q = q.reshape(B, S, DIFF_HEADS, 2, DIFF_QK)
    k = k.reshape(B, S, DIFF_HEADS, 2, DIFF_QK)
    v = v.reshape(B, S, DIFF_HEADS, DIFF_V)
    lamf = lam.astype(jnp.float32)
    lam_full = (jnp.exp(jnp.sum(lamf[0] * lamf[1])) - jnp.exp(jnp.sum(lamf[2] * lamf[3]))
                + lam_init)
    scale = DIFF_QK ** -0.5
    posf = pos.astype(jnp.float32)

    def block(i):
        start = i * Q_BLOCK
        qb = lax.dynamic_slice_in_dim(q, start, Q_BLOCK, axis=1)
        pq = lax.dynamic_slice_in_dim(posf, start, Q_BLOCK, axis=1)
        s = jnp.einsum('bqhmd,bkhmd->bmhqk', qb, k).astype(jnp.float32) * scale
        dist = jnp.abs(pq[:, :, None] - posf[:, None, :])
        s = s - slopes[None, None, :, None, None] * dist[:, None, None]
        s = jnp.where(chunk_causal_mask(start, S), s, -jnp.inf)
        p = jax.nn.softmax(s, axis=-1)
        a = p[:, 0] - lam_full * p[:, 1]
        return jnp.einsum('bhqk,bkhd->bqhd', a.astype(v.dtype), v)

    o = sweep_query_blocks(block, S)
    o = rms_norm(o, sub_norm.reshape(DIFF_HEADS, DIFF_V)) * (1.0 - lam_init)
    return o.reshape(B, S, DIFF_WIDTH)

def chunk_attention(h, rel_bias):
    B, S, _ = h.shape
    nc = S // CHUNK
    q, k, v = [t.reshape(B, nc, CHUNK, CH_HEADS, CH_HD) for t in jnp.split(h, 3, axis=-1)]
    band_idx = jnp.arange(nc)[:, None] + jnp.arange(CH_LEFT + 1)[None, :]

    def band(t):
        tp = jnp.pad(t, ((0, 0), (CH_LEFT, 0), (0, 0), (0, 0), (0, 0)))
        return tp[:, band_idx].reshape(B, nc, CH_BAND, CH_HEADS, CH_HD)

    kb, vb = band(k), band(v)
    s = jnp.einsum('bnqhd,bnkhd->bnhqk', q, kb).astype(jnp.float32) * (CH_HD ** -0.5)
    rel = (CH_LEFT * CHUNK + jnp.arange(CHUNK))[:, None] - jnp.arange(CH_BAND)[None, :]
    rel_idx = jnp.clip(rel, -(CHUNK - 1), REL_MAX) + (CHUNK - 1)
    bias = rel_bias[:, rel_idx].astype(jnp.float32)
    key_chunk = jnp.arange(nc)[:, None] - CH_LEFT + (jnp.arange(CH_BAND) // CHUNK)[None, :]
    valid = key_chunk >= 0
    s = jnp.where(valid[None, :, None, None, :], s + bias[None, None], -jnp.inf)
    p = jax.nn.softmax(s, axis=-1)
    o = jnp.einsum('bnhqk,bnkhd->bnqhd', p.astype(vb.dtype), vb)
    return o.reshape(B, S, CH_WIDTH)

def conv_ffn(x, w_in, conv_w, conv_b, w_out):
    h = x @ w_in
    c = h.shape[-1]
    h = lax.conv_general_dilated(h, conv_w[:, None, :].astype(h.dtype), window_strides=(1,),
                                 padding=[(CONV_W - 1, 0)],
                                 dimension_numbers=('NWC', 'WIO', 'NWC'),
                                 feature_group_count=c) + conv_b
    u, g = jnp.split(h, 2, axis=-1)
    return (jax.nn.silu(g) * u) @ w_out

def first_inputs(seed: int = 0) -> dict:
    key = jax.random.key(seed)
    ks = jax.random.split(key, 24)
    L, D = DEPTH, D_MODEL
    f32 = jnp.float32

    def w(k, shape, fan_in):
        return jax.random.normal(k, shape, f32) * fan_in ** -0.5

    def gain(k, shape):
        return 1.0 + 0.01 * jax.random.normal(k, shape, f32)

    x = jax.random.normal(ks[0], (BATCH, SEQ, D), f32)
    offsets = jax.random.randint(ks[1], (BATCH, 1), 0, 4096, dtype=jnp.int32)
    positions = offsets + jnp.arange(SEQ, dtype=jnp.int32)[None, :]
    return {
        'x': x,
        'positions': positions,
        'attn_norm': gain(ks[2], (L, D)),
        'w_in': w(ks[3], (L, D, IN_WIDTH), D),
        'mla_q_norm': gain(ks[4], (L, MLA_Q_RANK)),
        'mla_w_uq': w(ks[5], (L, MLA_Q_RANK, MLA_HEADS * (MLA_NOPE + MLA_ROPE)), MLA_Q_RANK),
        'mla_kv_norm': gain(ks[6], (L, MLA_KV_RANK)),
        'mla_w_ukv': w(ks[7], (L, MLA_KV_RANK, MLA_HEADS * (MLA_NOPE + MLA_V)), MLA_KV_RANK),
        'diff_lambda': 0.1 * jax.random.normal(ks[8], (L, 4, DIFF_QK), f32),
        'diff_norm': gain(ks[9], (L, DIFF_WIDTH)),
        'chunk_rel_bias': 0.1 * jax.random.normal(ks[10], (L, CH_HEADS, N_REL), f32),
        'mla_out_norm': gain(ks[11], (L, MLA_WIDTH)),
        'chunk_out_norm': gain(ks[12], (L, CH_WIDTH)),
        'w_out': w(ks[13], (L, MIX_WIDTH, D), MIX_WIDTH),
        'ffn_norm': gain(ks[14], (L, D)),
        'w_ffn_in': w(ks[15], (L, D, 2 * D_FF), D),
        'ffn_conv_w': w(ks[16], (L, CONV_W, 2 * D_FF), CONV_W),
        'ffn_conv_b': 0.01 * jax.random.normal(ks[17], (L, 2 * D_FF), f32),
        'w_ffn_out': w(ks[18], (L, D_FF, D), D_FF),
        'final_norm': gain(ks[19], (D,)),
    }

def first_block(x, positions, attn_norm, w_in, mla_q_norm, mla_w_uq, mla_kv_norm, mla_w_ukv,
              diff_lambda, diff_norm, chunk_rel_bias, mla_out_norm, chunk_out_norm, w_out,
              ffn_norm, w_ffn_in, ffn_conv_w, ffn_conv_b, w_ffn_out, final_norm):
    slopes = alibi_slopes(DIFF_HEADS)
    for l in range(DEPTH):
        lam_init = 0.8 - 0.6 * math.exp(-0.3 * l)
        proj = rms_norm(x, attn_norm[l]) @ w_in[l]
        h_mla, h_diff, h_ch = jnp.split(proj, [IN_MLA, IN_MLA + IN_DIFF], axis=-1)
        o_mla = rms_norm(mla_attention(h_mla, positions, mla_q_norm[l], mla_w_uq[l],
                                       mla_kv_norm[l], mla_w_ukv[l]), mla_out_norm[l])
        o_diff = diff_attention(h_diff, positions, diff_lambda[l], diff_norm[l], lam_init, slopes)
        o_ch = rms_norm(chunk_attention(h_ch, chunk_rel_bias[l]), chunk_out_norm[l])
        x = x + jnp.concatenate([o_mla, o_diff, o_ch], axis=-1) @ w_out[l]
        x = x + conv_ffn(rms_norm(x, ffn_norm[l]), w_ffn_in[l], ffn_conv_w[l], ffn_conv_b[l],
                         w_ffn_out[l])
    return rms_norm(x, final_norm)


DEPTH_2 = 1

N_HEADS_ATTN = 8
HEAD_DIM = 64
D_ATTN = N_HEADS_ATTN * HEAD_DIM
D_SSM = D_MODEL // 2
SSM_GROUP = 16
N_SSM_GROUPS = D_SSM // SSM_GROUP
SSM_STATE = 64
DT_MIN = 1e-3
DT_MAX = 1e-1
N_EXPERT_GROUPS = 4
EXPERTS_PER_GROUP = 8
N_EXPERTS = N_EXPERT_GROUPS * EXPERTS_PER_GROUP
TOP_K = 2
D_EXPERT = D_MODEL // 4
D_IN_PROJ = 3 * D_ATTN + N_HEADS_ATTN + D_SSM + 2 * D_MODEL
NEG_INF = -1e30


def _rmsnorm(x, g):
    xf = x.astype(jnp.float32)
    y = xf * lax.rsqrt(jnp.mean(xf * xf, axis=-1, keepdims=True) + EPS)
    return (y * g.astype(jnp.float32)).astype(x.dtype)

def _forgetting_attention(q, k, v, f_logit):
    b, s, h, d = q.shape
    n_blk = s // Q_BLOCK
    log_f = jax.nn.log_sigmoid(f_logit.astype(jnp.float32))
    cum = jnp.cumsum(log_f, axis=1).transpose(0, 2, 1)
    qf = q.astype(jnp.float32).transpose(0, 2, 1, 3) * (d ** -0.5)
    kf = k.astype(jnp.float32).transpose(0, 2, 1, 3)
    vf = v.astype(jnp.float32).transpose(0, 2, 1, 3)
    q_blk = qf.reshape(b, h, n_blk, Q_BLOCK, d).transpose(2, 0, 1, 3, 4)
    c_blk = cum.reshape(b, h, n_blk, Q_BLOCK).transpose(2, 0, 1, 3)
    pos = jnp.arange(s, dtype=jnp.int32)
    p_blk = pos.reshape(n_blk, Q_BLOCK)

    def one_block(args):
        qb, cb, pb = args
        logits = jnp.einsum('bhqd,bhkd->bhqk', qb, kf) + cb[..., :, None] - cum[:, :, None, :]
        causal = pos[None, :] <= pb[:, None]
        logits = jnp.where(causal, logits, NEG_INF)
        p = jax.nn.softmax(logits, axis=-1)
        return jnp.einsum('bhqk,bhkd->bhqd', p, vf)

    o = lax.map(one_block, (q_blk, c_blk, p_blk))
    return o.transpose(1, 0, 3, 2, 4).reshape(b, s, h, d).astype(v.dtype)

def _linear_combine(a, b):
    a1, b1 = a
    a2, b2 = b
    return a2 * a1, a2 * b1 + b2

def _s5(u, A_re, A_im, log_dt, B_re, B_im, C_re, C_im, D_skip, w_glu):
    f32 = jnp.float32
    b, s, _ = u.shape
    uf = u.astype(f32).reshape(b, s, N_SSM_GROUPS, SSM_GROUP)
    A = lax.complex(A_re.astype(f32), A_im.astype(f32))
    dt = jnp.exp(log_dt.astype(f32))[:, None]
    A_bar = jnp.exp(A * dt)
    Bm = lax.complex(B_re.astype(f32), B_im.astype(f32))
    B_bar = ((A_bar - 1.0) / A)[..., None] * Bm
    Bu = jnp.einsum('bsgc,gpc->bsgp', uf.astype(jnp.complex64), B_bar)
    A_seq = jnp.broadcast_to(A_bar, Bu.shape)
    _, state = lax.associative_scan(_linear_combine, (A_seq, Bu), axis=1)
    Cm = lax.complex(C_re.astype(f32), C_im.astype(f32))
    y = jnp.real(jnp.einsum('gcp,bsgp->bsgc', Cm, state))
    y = y + D_skip.astype(f32).reshape(N_SSM_GROUPS, SSM_GROUP) * uf
    y = jax.nn.gelu(y.reshape(b, s, D_SSM))
    y = y * jax.nn.sigmoid(y @ w_glu.astype(f32))
    return y.astype(u.dtype)

def _hier_moe(x, w_rg, b_rg, w_re, b_re, w_gate, w_up, w_down):
    f32 = jnp.float32
    b, s, d = x.shape
    t = b * s
    xt = x.reshape(t, d)
    g_prob = jax.nn.softmax((xt @ w_rg).astype(f32) + b_rg.astype(f32), axis=-1)
    g_top, g_sel = lax.top_k(g_prob, 1)
    e_logits = ((xt @ w_re).astype(f32) + b_re.astype(f32)).reshape(t, N_EXPERT_GROUPS, EXPERTS_PER_GROUP)
    idx = jnp.broadcast_to(g_sel[:, :, None], (t, 1, EXPERTS_PER_GROUP))
    e_in = jnp.take_along_axis(e_logits, idx, axis=1)[:, 0]
    e_prob = jax.nn.softmax(e_in, axis=-1)
    e_top, e_idx = lax.top_k(e_prob, TOP_K)
    w = g_top * e_top / jnp.sum(e_top, axis=-1, keepdims=True)
    expert_id = g_sel * EXPERTS_PER_GROUP + e_idx
    combine = jnp.sum(jax.nn.one_hot(expert_id, N_EXPERTS, dtype=f32) * w[..., None], axis=1).astype(x.dtype)
    y = jnp.zeros_like(xt)
    for e in range(N_EXPERTS):
        h = jax.nn.silu(xt @ w_gate[e]) * (xt @ w_up[e])
        y = y + combine[:, e:e + 1] * (h @ w_down[e])
    return y.reshape(b, s, d)

def second_inputs(seed: int = 0) -> dict:
    key = jax.random.key(seed)
    ks = jax.random.split(key, 32)
    f32 = jnp.float32
    nrm = lambda k, shape, scale: (jax.random.normal(k, shape, f32) * scale)
    L = DEPTH_2
    x = jax.random.normal(ks[0], (BATCH, SEQ, D_MODEL), f32)
    norm_mix_g = 1.0 + nrm(ks[1], (L, D_MODEL), 0.02)
    w_in = nrm(ks[2], (L, D_MODEL, D_IN_PROJ), D_MODEL ** -0.5)
    b_forget = jnp.broadcast_to(jnp.linspace(1.0, 6.0, N_HEADS_ATTN, dtype=f32), (L, N_HEADS_ATTN)) + nrm(ks[3], (L, N_HEADS_ATTN), 0.1)
    q_norm_g = 1.0 + nrm(ks[4], (L, HEAD_DIM), 0.02)
    k_norm_g = 1.0 + nrm(ks[5], (L, HEAD_DIM), 0.02)
    ssm_A_re = -0.5 + nrm(ks[6], (L, N_SSM_GROUPS, SSM_STATE), 0.01)
    ssm_A_im = jnp.pi * jnp.arange(SSM_STATE, dtype=f32)[None, None, :] + nrm(ks[7], (L, N_SSM_GROUPS, SSM_STATE), 0.01)
    ssm_log_dt = jax.random.uniform(ks[8], (L, N_SSM_GROUPS), f32, math.log(DT_MIN), math.log(DT_MAX))
    ssm_B_re = nrm(ks[9], (L, N_SSM_GROUPS, SSM_STATE, SSM_GROUP), (2 * SSM_GROUP) ** -0.5)
    ssm_B_im = nrm(ks[10], (L, N_SSM_GROUPS, SSM_STATE, SSM_GROUP), (2 * SSM_GROUP) ** -0.5)
    ssm_C_re = nrm(ks[11], (L, N_SSM_GROUPS, SSM_GROUP, SSM_STATE), (2 * SSM_STATE) ** -0.5)
    ssm_C_im = nrm(ks[12], (L, N_SSM_GROUPS, SSM_GROUP, SSM_STATE), (2 * SSM_STATE) ** -0.5)
    ssm_D = nrm(ks[13], (L, D_SSM), 1.0)
    w_glu = nrm(ks[14], (L, D_SSM, D_SSM), D_SSM ** -0.5)
    w_proj_attn = nrm(ks[15], (L, D_ATTN, D_MODEL), D_ATTN ** -0.5)
    w_proj_ssm = nrm(ks[16], (L, D_SSM, D_MODEL), D_SSM ** -0.5)
    w_out = nrm(ks[17], (L, D_MODEL, D_MODEL), D_MODEL ** -0.5)
    norm_ffn_g = 1.0 + nrm(ks[18], (L, D_MODEL), 0.02)
    w_router_group = nrm(ks[19], (L, D_MODEL, N_EXPERT_GROUPS), D_MODEL ** -0.5)
    b_router_group = nrm(ks[20], (L, N_EXPERT_GROUPS), 0.01)
    w_router_expert = nrm(ks[21], (L, D_MODEL, N_EXPERTS), D_MODEL ** -0.5)
    b_router_expert = nrm(ks[22], (L, N_EXPERTS), 0.01)
    w_expert_gate = nrm(ks[23], (L, N_EXPERTS, D_MODEL, D_EXPERT), D_MODEL ** -0.5)
    w_expert_up = nrm(ks[24], (L, N_EXPERTS, D_MODEL, D_EXPERT), D_MODEL ** -0.5)
    w_expert_down = nrm(ks[25], (L, N_EXPERTS, D_EXPERT, D_MODEL), D_EXPERT ** -0.5)
    return {"x": x, "norm_mix_g": norm_mix_g, "w_in": w_in, "b_forget": b_forget,
            "q_norm_g": q_norm_g, "k_norm_g": k_norm_g,
            "ssm_A_re": ssm_A_re, "ssm_A_im": ssm_A_im, "ssm_log_dt": ssm_log_dt,
            "ssm_B_re": ssm_B_re, "ssm_B_im": ssm_B_im, "ssm_C_re": ssm_C_re, "ssm_C_im": ssm_C_im,
            "ssm_D": ssm_D, "w_glu": w_glu, "w_proj_attn": w_proj_attn, "w_proj_ssm": w_proj_ssm,
            "w_out": w_out, "norm_ffn_g": norm_ffn_g,
            "w_router_group": w_router_group, "b_router_group": b_router_group,
            "w_router_expert": w_router_expert, "b_router_expert": b_router_expert,
            "w_expert_gate": w_expert_gate, "w_expert_up": w_expert_up, "w_expert_down": w_expert_down}

def second_block(x, norm_mix_g, w_in, b_forget, q_norm_g, k_norm_g,
              ssm_A_re, ssm_A_im, ssm_log_dt, ssm_B_re, ssm_B_im, ssm_C_re, ssm_C_im,
              ssm_D, w_glu, w_proj_attn, w_proj_ssm, w_out, norm_ffn_g,
              w_router_group, b_router_group, w_router_expert, b_router_expert,
              w_expert_gate, w_expert_up, w_expert_down):
    b, s, _ = x.shape
    splits = np.cumsum([D_ATTN, D_ATTN, D_ATTN, N_HEADS_ATTN, D_SSM, D_MODEL]).tolist()
    for l in range(DEPTH_2):
        h = _rmsnorm(x, norm_mix_g[l])
        z = h @ w_in[l]
        q, k, v, f, u_ssm, g_attn, g_ssm = jnp.split(z, splits, axis=-1)
        q = _rmsnorm(q.reshape(b, s, N_HEADS_ATTN, HEAD_DIM), q_norm_g[l])
        k = _rmsnorm(k.reshape(b, s, N_HEADS_ATTN, HEAD_DIM), k_norm_g[l])
        v = v.reshape(b, s, N_HEADS_ATTN, HEAD_DIM)
        y_attn = _forgetting_attention(q, k, v, f + b_forget[l]).reshape(b, s, D_ATTN)
        y_ssm = _s5(u_ssm, ssm_A_re[l], ssm_A_im[l], ssm_log_dt[l], ssm_B_re[l], ssm_B_im[l],
                    ssm_C_re[l], ssm_C_im[l], ssm_D[l], w_glu[l])
        mixed = (jax.nn.sigmoid(g_attn) * (y_attn @ w_proj_attn[l])
                 + jax.nn.sigmoid(g_ssm) * (y_ssm @ w_proj_ssm[l]))
        x = x + mixed @ w_out[l]
        x = x + _hier_moe(_rmsnorm(x, norm_ffn_g[l]), w_router_group[l], b_router_group[l],
                          w_router_expert[l], b_router_expert[l],
                          w_expert_gate[l], w_expert_up[l], w_expert_down[l])
    return x


def setup_inputs(seed=0):
    out = dict(first_inputs(seed))
    for name, value in second_inputs(seed + 1).items():
        if name != "x":
            out[name + "_2"] = value
    return out


def reference(
    x, positions, attn_norm, w_in, mla_q_norm, mla_w_uq, mla_kv_norm, mla_w_ukv, diff_lambda,
    diff_norm, chunk_rel_bias, mla_out_norm, chunk_out_norm, w_out, ffn_norm, w_ffn_in,
    ffn_conv_w, ffn_conv_b, w_ffn_out, final_norm, norm_mix_g_2, w_in_2, b_forget_2, q_norm_g_2,
    k_norm_g_2, ssm_A_re_2, ssm_A_im_2, ssm_log_dt_2, ssm_B_re_2, ssm_B_im_2, ssm_C_re_2,
    ssm_C_im_2, ssm_D_2, w_glu_2, w_proj_attn_2, w_proj_ssm_2, w_out_2, norm_ffn_g_2,
    w_router_group_2, b_router_group_2, w_router_expert_2, b_router_expert_2, w_expert_gate_2,
    w_expert_up_2, w_expert_down_2,
):
    x = first_block(
        x, positions, attn_norm, w_in, mla_q_norm, mla_w_uq, mla_kv_norm, mla_w_ukv,
        diff_lambda, diff_norm, chunk_rel_bias, mla_out_norm, chunk_out_norm, w_out, ffn_norm,
        w_ffn_in, ffn_conv_w, ffn_conv_b, w_ffn_out, final_norm,
    )
    return second_block(
        x, norm_mix_g_2, w_in_2, b_forget_2, q_norm_g_2, k_norm_g_2, ssm_A_re_2, ssm_A_im_2,
        ssm_log_dt_2, ssm_B_re_2, ssm_B_im_2, ssm_C_re_2, ssm_C_im_2, ssm_D_2, w_glu_2,
        w_proj_attn_2, w_proj_ssm_2, w_out_2, norm_ffn_g_2, w_router_group_2, b_router_group_2,
        w_router_expert_2, b_router_expert_2, w_expert_gate_2, w_expert_up_2, w_expert_down_2,
    )


_drawn_inputs = setup_inputs


def setup_inputs(seed=0):
    import zlib

    import numpy as np

    out = dict(_drawn_inputs(seed))
    spreads = {}
    factors = {'mla_q_norm': 3.001,
     'mla_kv_norm': 2.957,
     'diff_norm': 3.172,
     'mla_out_norm': 2.887,
     'chunk_out_norm': 4.49,
     'norm_mix_g_2': 2.827,
     'q_norm_g_2': 7.855,
     'k_norm_g_2': 5.667,
     'ssm_A_re_2': 64.0,
     'ssm_B_im_2': 2.765,
     'ssm_C_re_2': 2.673,
     'b_router_group_2': 29.057,
     'b_router_expert_2': 8.0,
     'ssm_C_im_2': 2.835,
     'norm_ffn_g_2': 3.905}
    for name, (base, spread) in spreads.items():
        noise = np.random.default_rng([zlib.crc32(name.encode()), seed]).standard_normal(out[name].shape)
        drawn = base * np.exp(spread * noise) if base else spread * noise
        out[name] = __import__('jax').numpy.asarray(drawn.astype(out[name].dtype))
    for name, factor in factors.items():
        out[name] = (out[name] * factor).astype(out[name].dtype)
    return out
```

```python
import math
from contextlib import ExitStack

import concourse.bass as bass
from concourse import mybir

F32 = mybir.dt.float32
F32R = mybir.dt.float32r
I32 = mybir.dt.int32
ALU = mybir.AluOpType
ACT = mybir.ActivationFunctionType
AX_X = mybir.AxisListType.X

P = 128
T = 512
D = 1024
KD = D // P
NQ = T // P
LAYERS = 2
EPS = 1e-6

Q_RANK, KV_RANK, NOPE, ROPE, MLA_H, MLA_V = 256, 128, 64, 32, 6, 64
DIFF_H, DIFF_QK, DIFF_V = 6, 32, 64
CH_H, CH_HD, CHUNK, REL_MAX = 4, 64, 64, 256
D_FF = 2816
JF = D_FF // P
MLA_SCALE = (NOPE + ROPE) ** -0.5
DIFF_SCALE = DIFF_QK ** -0.5
CH_SCALE = CH_HD ** -0.5
MASKED = -1e30
HIGH_BITS = -(1 << 12)
VCOLS = DIFF_H * DIFF_V + CH_H * CH_HD

SLOT = 2 * KD * P
RING = 3
FEATURE_BLOCKS = 7
TOKEN_BLOCKS = 3
BLOCKS_PROJ = FEATURE_BLOCKS + TOKEN_BLOCKS
BLOCKS_MLA = 2
BLOCKS_OUT = 4
BLOCKS_FFN_IN = JF
BLOCKS_FFN_OUT = 2 * KD
BLOCK_MLA = BLOCKS_PROJ
BLOCK_OUT = BLOCK_MLA + BLOCKS_MLA
BLOCK_FFN_IN = BLOCK_OUT + BLOCKS_OUT
BLOCK_FFN_OUT = BLOCK_FFN_IN + BLOCKS_FFN_IN
LAYER_BLOCKS = BLOCK_FFN_OUT + BLOCKS_FFN_OUT
assert LAYER_BLOCKS % RING == 0
BODY = 2 * RING
SPLIT_FFN = BLOCKS_PROJ + BLOCKS_OUT
SPLIT_OUT = SPLIT_FFN + JF
SPLITS = SPLIT_OUT + BLOCKS_FFN_OUT
H_HIGH_AT = 33
EARLY = H_HIGH_AT - JF - 6
assert EARLY + 2 * KD + 1 == JF
assert BLOCKS_PROJ % 2 == 0 and BLOCKS_OUT % 2 == 0 and H_HIGH_AT >= JF + 6

PAR = {}
_at = 0
for _name, _n in (("attn_norm", KD), ("ffn_norm", KD), ("q_norm", 2), ("kv_norm", 1), ("mla_out", 3), ("diff_norm", 3),
                  ("chunk_out", 2), ("conv_w", 3 * 2 * JF), ("conv_b", 2 * JF), ("lam", 4 * DIFF_QK),
                  ("lam_init", 1), ("one_minus_lam_init", 1)):
    PAR[_name] = (_at, _at + _n)
    _at += _n
PAR_W = _at
CON = {}
_at = 0
for _name, _n in (("ident", P), ("ones", P), ("block64", P), ("inv_freq", 1), ("phase", 1), ("sign", 1), ("eps", 1),
                  ("final_norm", KD), ("mask", P)):
    CON[_name] = (_at, _at + _n)
    _at += _n
CON_W = _at

SLOPES = [2.0 ** (-8.0 * (h + 1) / DIFF_H) for h in range(DIFF_H)]

MAPS = ([("mla", h, 0, i) for h in range(MLA_H) for i in range(NQ)]
        + [("diff", h, m, i) for h in range(DIFF_H) for i in range(NQ) for m in range(2)]
        + [("chunk", h, 0, i) for h in range(CH_H) for i in range(NQ)])
PBLOCKS = []
for _u, (_k, _h, _m, _i) in enumerate(MAPS):
    if _m == 0:
        PBLOCKS.append([_k, _h, _i, [_u]])
    else:
        PBLOCKS[-1][3].append(_u)
PBLOCK_OF = {u: t for t, b in enumerate(PBLOCKS) for u in b[3]}
HEADS = MLA_H + DIFF_H + CH_H
NMAPS = len(MAPS)
NPB = len(PBLOCKS)
assert NPB == HEADS * NQ
PBUF = 6
SCORE_BANKS = (0, 1, 2, 7)
NSB = len(SCORE_BANKS)
LAG = 2


def attention_order():
    order = []
    scored = 0
    for t in range(NPB + LAG + 1):
        while scored < NMAPS and (t >= NPB or scored <= max(PBLOCKS[min(t, NPB - 1)][3])):
            order.append(("scores", scored))
            scored += 1
        if LAG <= t < NPB + LAG:
            order.append(("turn", t - LAG))
        if t > LAG and (t - LAG - 1) % NQ == NQ - 1:
            order.append(("heads", (t - LAG - 1) // NQ))
    return order


def layer_outputs():
    out = [("norm", 0)]
    out += [("feature", t) for t in range(2 * FEATURE_BLOCKS)]
    out += [("sum_q", 0), ("sum_kv", 0)]
    out += [("token", b, c) for b in range(TOKEN_BLOCKS) for c in range(NQ)]
    out += [("uq", h) for h in range(MLA_H)] + [("uk", h) for h in range(MLA_H)] + [("uv", c) for c in range(NQ)]
    out += attention_order()
    out += [("out_norm", n) for n in range(5)]
    out += [("w_out", m) for m in range(KD)]
    out += [("norm", 1)]
    out += [("ffn_in", j, s) for j in range(JF) for s in range(2)]
    out += [(name, m) for m in range(KD) for name in ("ffn_half", "ffn_out")]
    return out


LAYER_OUT = layer_outputs()
PER_LAYER = len(LAYER_OUT)
PLACE = {name: n + 1 for n, name in enumerate(LAYER_OUT)}


def done(l, *name):
    return l * PER_LAYER + (PER_LAYER + PLACE[name])


def last_use(n):
    if n < FEATURE_BLOCKS:
        return "feature", 2 * n + 1
    if n < BLOCK_MLA:
        return "token", n - FEATURE_BLOCKS, NQ - 1
    if n < BLOCK_OUT:
        return [("uq", MLA_H - 1), ("uv", NQ - 1)][n - BLOCK_MLA]
    if n < BLOCK_FFN_IN:
        return "w_out", 2 * (n - BLOCK_OUT) + 1
    if n < BLOCK_FFN_OUT:
        return "ffn_in", n - BLOCK_FFN_IN, 1
    return ("ffn_half", "ffn_out")[(n - BLOCK_FFN_OUT) % 2], (n - BLOCK_FFN_OUT) // 2


def block_words(n):
    if n == FEATURE_BLOCKS + 2:
        return KD * P
    if n == BLOCK_MLA:
        return 2 * MLA_H * P
    if n == BLOCK_MLA + 1:
        return 2 * MLA_H * MLA_V
    if n >= BLOCK_FFN_OUT:
        return JF // 2 * P
    return SLOT


FH, FD = 8, 64
SSM = D // 2
SG, SC, SN = 32, 16, 64
ST = SG * SN // P
YT = SSM // P
EG, EPG = 4, 8
NE = EG * EPG
DE = D // 4
NR = EG + NE
BIG = 1e30
U32 = mybir.dt.uint32
HROWS = FD + 2
MAX_BLOCKS = NE + T * 2 // P
MAX_PAIRS = MAX_BLOCKS // 2

CON2 = {}
_at = 0
for _name, _n in (("mix_norm", KD), ("ffn_norm", KD), ("q_gain", 1), ("k_gain", 1), ("b_forget", 1), ("d_skip", YT),
                  ("a_re", ST), ("a_im", ST), ("log_dt", ST), ("w_f", KD * FH), ("w_router", KD * NR), ("b_router", NR),
                  ("causal", P), ("before", P), ("token", NQ), ("index", MAX_BLOCKS)):
    CON2[_name] = (_at, _at + _n)
    _at += _n
CON2_W = _at

B2_U, B2_Q, B2_K, B2_V = 0, 2, 4, 6
B2_S = 8
B2_GLU = B2_S + 3 * YT
B2_PSSM = B2_GLU + 1
B2_PATTN = B2_PSSM + 2
B2_OUT = B2_PATTN + 2
B2_MOE = B2_OUT + 4
RING0 = LAYERS * LAYER_BLOCKS // RING * 16
assert LAYERS * LAYER_BLOCKS % RING == 0


def attention2_order():
    order = []
    for t in range(FH * NQ + LAG + 1):
        if t < FH * NQ:
            order.append(("scores2", t))
        if LAG <= t < FH * NQ + LAG:
            order.append(("turn2", t - LAG))
        if t > LAG and (t - LAG - 1) % NQ == NQ - 1:
            order.append(("heads2", (t - LAG - 1) // NQ))
    return order


def second_outputs():
    out = [("norm2", 0), ("norm2", 1)]
    out += [("u", t) for t in range(YT)] + [("f", 0)]
    out += [("q", t) for t in range(4)] + [("k", t) for t in range(4)]
    out += [("qk_sum", t) for t in range(8)]
    out += [("v", b, c) for b in range(2) for c in range(NQ)]
    for st in range(ST + 1):
        if st < ST:
            out += [("B", st, 0), ("B", st, 1), ("g", st)]
        if st:
            out.append(("C", st - 1))
    out += [("glu", m) for m in range(YT)] + [("pssm", m) for m in range(KD)]
    out += attention2_order()
    out += [("pattn", m) for m in range(KD)] + [("w_out2", m) for m in range(KD)]
    out += [("norm2", 2)]
    out += [("router", c) for c in range(NQ)] + [("rank", c) for c in range(NQ)] + [("count", 0)]
    out += [("ht", n) for n in range(2 * NQ)] + [("xt", n) for n in range(2 * NQ)]
    return out


SECOND_OUT = second_outputs()
PLACE2 = {name: n + 1 for n, name in enumerate(SECOND_OUT)}
SECOND0 = (LAYERS + 1) * PER_LAYER


def done2(*name):
    return SECOND0 + PLACE2[name]


EXPERT_STEPS = [("x_turn", 0, 0), ("x_turn", 0, 1), ("gate", 0), ("up", 0), ("x_turn", 1, 0), ("x_turn", 1, 1),
                ("lacking", 0), ("lacking", 1)]
for _e in range(1, NE):
    EXPERT_STEPS += [("h_turn", _e - 1), ("gate", _e), ("up", _e), ("x_turn", _e + 1, 0), ("x_turn", _e + 1, 1),
                     ("down", _e - 1, 0), ("down", _e - 1, 1)]
PLACE3 = {name: n + 1 for n, name in enumerate(EXPERT_STEPS)}
EXPERTS0 = SECOND0 + len(SECOND_OUT)
PER_EXPERT = 7


def done3(name, e, *rest):
    if isinstance(e, int):
        return EXPERTS0 + PLACE3[(name, e, *rest)]
    return e * PER_EXPERT + (EXPERTS0 + PLACE3[(name, 1, *rest)] - PER_EXPERT)


def last_use2(n):
    if n < B2_Q:
        return "u", 2 * n + 1
    if n < B2_K:
        return "q", 2 * (n - B2_Q) + 1
    if n < B2_V:
        return "k", 2 * (n - B2_K) + 1
    if n < B2_S:
        return "v", n - B2_V, NQ - 1
    if n < B2_GLU:
        a, r = divmod(n - B2_S, 3)
        return ("B", 4 * a + 3, 1) if r == 0 else ("g", 4 * a + 2 * r - 1)
    if n < B2_PSSM:
        return "glu", YT - 1
    if n < B2_PATTN:
        return "pssm", 4 * (n - B2_PSSM) + 3
    if n < B2_OUT:
        return "pattn", 4 * (n - B2_PATTN) + 3
    return "w_out2", 2 * (n - B2_OUT) + 1


OUT_NORM_TILES = [(0, 3), (3, 4), (4, 5), (5, 6), (6, 8)]


def build(nc, a, out):
    with ExitStack() as ctx:
        def sb(name, shape, dt=F32):
            return ctx.enter_context(nc.sbuf_tensor(name, shape, dt))

        def sem(name):
            return ctx.enter_context(nc.semaphore(name))

        def second_names(*parts):
            with ExitStack() as place:
                return [place.enter_context(nc.sbuf_tensor(name, shape, dt)) for name, shape, dt in parts]

        x = sb("x", [P, KD, T])
        (h_low,) = second_names(("h_low", [P, KD, T], F32R))
        h = sb("h", [P, KD, T])
        w_low = second_names(*[(f"w_low{s}", [P, SLOT], F32R) for s in range(RING)])
        ring = [sb(f"ring{s}", [P, SLOT]) for s in range(RING)]
        con = sb("con", [P, CON_W])
        par = sb("par", [P, PAR_W])
        con2 = sb("con2", [P, CON2_W])
        w_high = second_names(("before_w_high", [P, 6 * T], F32), *[(f"w_high{n}", [P, SLOT], F32R) for n in range(2)])[1:]
        extra = sb("extra", [P, (4 + 1 + 1 + 4 + PBUF) * T + P * NQ * (NQ + 1) // 2])
        rel = extra[:, 0:CH_H * T].rearrange("p (h t) -> p h t", h=CH_H)
        trig = extra[:, 4 * T:5 * T]
        pos_i = extra[:, 5 * T:6 * T].bitcast(I32)
        probs = extra[:, 6 * T:(6 + PBUF) * T].rearrange("p (b t) -> p b t", b=PBUF)
        tmp = [extra[:, (6 + PBUF + n) * T:(7 + PBUF + n) * T] for n in range(4)]
        dist = extra[:, (10 + PBUF) * T:]
        w_part = [extra[:, 6 * T + n * SLOT:6 * T + (n + 1) * SLOT] for n in range(2)]
        posc_i = sb("posc_i", [P, NQ], I32)
        posc = sb("posc", [P, NQ])
        lam = sb("lam", [P, 8])
        lamp = sb("lamp", [P, 2 * DIFF_QK])
        gdiff = sb("gdiff", [P, 3])
        rstd = sb("rstd", [P, 2, T])
        stat = sb("stat", [P, 2, NMAPS])
        rsum = sb("rsum", [P, NMAPS])
        h_high = second_names(("before_h_high", [P, H_HIGH_AT * T], F32), ("h_high", [P, KD, T], F32R))[1]
        act_low, act_high_last, _, act_high_first = second_names(
            ("act_low", [P, JF, T], F32R), ("act_high_last", [P, T], F32R), ("between", [P, 5 * T], F32),
            ("act_high_first", [P, EARLY, T], F32R))
        work = sb("work", [P, 22 * 1024])
        h_part = work[:, H_HIGH_AT * T:(H_HIGH_AT + KD) * T].rearrange("p (k t) -> p k t", k=KD)
        used = [0]

        def part(words):
            used[0] += words
            assert used[0] <= 22 * 1024
            return work[:, used[0] - words:used[0]]

        qm = part(MLA_H * T).rearrange("p (h t) -> p h t", h=MLA_H)
        km = part(MLA_H * T).rearrange("p (h t) -> p h t", h=MLA_H)
        vm = part(NQ * MLA_H * MLA_V).rearrange("p (c v) -> p c v", c=NQ)
        cqkv = part(3 * T).rearrange("p (c t) -> p c t", c=3)
        qk = part(10 * T).rearrange("p (c t) -> p c t", c=10)
        vt = part(NQ * VCOLS).rearrange("p (c v) -> p c v", c=NQ)
        assert used[0] == H_HIGH_AT * T
        pt = [part(NQ * T).rearrange("p (c t) -> p c t", c=NQ) for _ in range(2)]
        sq3 = vm.rearrange("p c v -> p (c v)").rearrange("p (c t) -> p c t", c=3)
        rope_tmp = [pos_i.bitcast(F32), rstd[:, 0, :]]
        osq = work[:, 0:KD * T].rearrange("p (c t) -> p c t", c=KD)
        act_ff = work[:, 0:JF * T].rearrange("p (c t) -> p c t", c=JF)
        conv = [work[:, (JF + n) * T:(JF + n + 1) * T] for n in range(4)]
        sil = [work[:, (JF + 4 + n) * T:(JF + 5 + n) * T] for n in range(2)]
        orst = [work[:, (KD + n) * T:(KD + n + 1) * T] for n in range(5)]

        powers = [work[:, (41 + n) * T:(42 + n) * T] for n in range(2)]
        power_tmp = [work[:, 43 * T:43 * T + T // 2], work[:, 43 * T + T // 2:44 * T]]
        s5 = sb("s5", [P, 20, ST])
        s5r, s5cr, s5ci, s5nci, s5ang, s5sc, s5a, s5b, s5den, s5t = (
            s5[:, 0, :], s5[:, 1, :], s5[:, 2, :], s5[:, 3, :], s5[:, 4:6, :], s5[:, 6:8, :], s5[:, 8:10, :],
            s5[:, 10:12, :], s5[:, 12, :], s5[:, 13:15, :])
        vpow = sb("vpow", [P, 9, 2, ST])
        cmix = [sb(f"cmix{n}", [P, 4, P]) for n in range(2)]
        act_high = [act_high_first[:, n, :] for n in range(EARLY)] + [h_high[:, n, :] for n in range(KD)]
        act_high += [h_low[:, n, :] for n in range(KD)] + [act_high_last[:]]
        act_part = [work[:, (JF + 6 + n) * T:(JF + 7 + n) * T] for n in range(EARLY)] + [h_part[:, n, :] for n in range(KD)]
        act_part += [h[:, n, :] for n in range(KD)] + [conv[0]]
        used[0] = 0
        qa = part(FH * T).rearrange("p (h t) -> p h t", h=FH)
        ka = part(FH * T).rearrange("p (h t) -> p h t", h=FH)
        va = part(NQ * FH * FD).rearrange("p (c v) -> p c v", c=NQ)
        us = part(YT * T).rearrange("p (c t) -> p c t", c=YT)
        ys = part(YT * T).rearrange("p (c t) -> p c t", c=YT)
        gates = part(2 * KD * T).rearrange("p (c t) -> p c t", c=2 * KD)
        wtab = [extra[:, 2 * n * T:2 * (n + 1) * T].rearrange("p (c t) -> p c t", c=2) for n in range(2)]
        zs = [extra[:, (4 + 2 * n) * T:(6 + 2 * n) * T].rearrange("p (c t) -> p c t", c=2) for n in range(2)]
        cs = [extra[:, (8 + 4 * n) * T:(12 + 4 * n) * T].rearrange("p (c t) -> p c t", c=4) for n in range(2)]
        fg = [extra[:, n * T:(n + 1) * T] for n in range(5)]
        y5 = [rstd[:, 0, :], rstd[:, 1, :]]
        ptb = [extra[:, 4 * n * T:4 * (n + 1) * T].rearrange("p (c t) -> p c t", c=NQ) for n in range(2)]
        probs2 = extra[:, 8 * T:(8 + PBUF) * T].rearrange("p (b t) -> p b t", b=PBUF)
        used[0] = 0
        ht = part(NQ * D).rearrange("p (c d) -> p c d", c=NQ)
        xt = part(NQ * D).rearrange("p (c d) -> p c d", c=NQ)
        xg = [part(D) for _ in range(2)]
        xgt = [part(KD * P) for _ in range(2)]
        hh = [part(2 * DE).rearrange("p (c d) -> p c d", c=2) for _ in range(2)]
        hgt = [part(2 * P) for _ in range(2)]
        yo = [part(D) for _ in range(2)]
        yg = [part(D) for _ in range(2)] + [ht[:, tc, :] for tc in range(NQ)] + yo
        rt = sb("rt", [P, 12, NQ, NE])
        rs = sb("rs", [P, 24, NQ])
        logits = sb("logits", [P, NQ, NR])
        slot_i = sb("slot_i", [P, 4, NQ], U32)
        token_i = sb("token_i", [P, NQ], U32)
        zero_i = sb("zero_i", [P, MAX_BLOCKS], U32)
        lists = sb("lists", [P, MAX_BLOCKS], U32)
        list_now = [sb(f"list_now{n}", [P, 1], U32) for n in range(2)]
        ends = sb("ends", [P, 4, NE])
        plan = extra[:, 0:MAX_BLOCKS * NE].rearrange("p (b e) -> p b e", b=MAX_BLOCKS)
        plan_f = sb("plan_f", [P, MAX_BLOCKS])
        pairs_f = sb("pairs_f", [P, 2])
        expert_of = sb("expert_of", [P, MAX_BLOCKS], I32)
        pairs_i = sb("pairs_i", [P, 1], I32)
        powers_d = nc.dram_tensor("powers_d", [ST, P, 2 * T], F32, kind="Internal").ap()
        hrows_d = nc.dram_tensor("hrows_d", [T, D], F32, kind="Internal").ap()
        slots_d = nc.dram_tensor("slots_d", [P * MAX_BLOCKS, 1], U32, kind="Internal").ap()
        yrows_d = nc.dram_tensor("yrows_d", [MAX_BLOCKS * P, D], F32, kind="Internal").ap()

        bank = [ctx.enter_context(nc.psum_tensor(f"bank{b}", [P, T], F32)) for b in range(8)]

        def c(name, n=None):
            lo, hi = CON[name]
            return con[:, lo:hi] if n is None else con[:, lo + n:lo + n + 1]

        def c2(name, n=None):
            lo, hi = CON2[name]
            return con2[:, lo:hi] if n is None else con2[:, lo + n:lo + n + 1]

        def g(name, n):
            lo = PAR[name][0]
            return par[:, lo + n:lo + n + 1]

        pe_done = sem("pe_done")
        x_in = sem("x_in")
        con_in = sem("con_in")
        pos_in = sem("pos_in")
        par_in = sem("par_in")
        arrived = [sem(f"arrived{s}") for s in range(RING)]
        trig_angle = sem("trig_angle")
        trig_sin = sem("trig_sin")
        tables = sem("tables")
        squares = sem("squares")
        logs = sem("logs")
        rstd_ready = sem("rstd_ready")
        normed = sem("normed")
        feature_out = sem("feature_out")
        mla_squares = sem("mla_squares")
        mla_logs = sem("mla_logs")
        mla_rstd = sem("mla_rstd")
        mla_normed = sem("mla_normed")
        token_out = sem("token_out")
        roped = sem("roped")
        rope_step = sem("rope_step")
        uq_out = sem("uq_out")
        lam_step = sem("lam_step")
        lam_exp = sem("lam_exp")
        maxed = sem("maxed")
        biased = sem("biased")
        exped = sem("exped")
        inv_step = sem("inv_step")
        scaled = sem("scaled")
        turned = sem("turned")
        head_out = sem("head_out")
        out_squares = sem("out_squares")
        out_logs = sem("out_logs")
        out_rstd = sem("out_rstd")
        out_normed = sem("out_normed")
        x_added = sem("x_added")
        h_masked = sem("h_masked")
        h_lowered = sem("h_lowered")
        h_split = sem("h_split")
        w_masked = sem("w_masked")
        w_lowered = sem("w_lowered")
        w_split = sem("w_split")
        act_masked = sem("act_masked")
        act_lowered = sem("act_lowered")
        act_split = sem("act_split")
        conv_base = sem("conv_base")
        conv_step = sem("conv_step")
        conv_done = sem("conv_done")
        silued = sem("silued")
        ffn_act = sem("ffn_act")
        layer_end = sem("layer_end")
        stored = sem("stored")
        s5_step = sem("s5_step")
        s5_act = sem("s5_act")
        powers_step = sem("powers_step")
        powers_out = sem("powers_out")
        powers_in = [sem(f"powers_in{n}") for n in range(2)]
        u_out = sem("u_out")
        f_out = sem("f_out")
        f_step = sem("f_step")
        cum_in = sem("cum_in")
        qk_raw = sem("qk_raw")
        qk_sq = sem("qk_sq")
        qk_log = sem("qk_log")
        qk_rst = sem("qk_rst")
        qk_norm = sem("qk_norm")
        v_out = sem("v_out")
        g_out = sem("g_out")
        z_ready = sem("z_ready")
        z_step = sem("z_step")
        rotated = sem("rotated")
        cmix_step = sem("cmix_step")
        cmixed = sem("cmixed")
        y_step = sem("y_step")
        y_sig = sem("y_sig")
        gelued = sem("gelued")
        glu_sig = sem("glu_sig")
        glued = sem("glued")
        ssm_mixed = sem("ssm_mixed")
        maxed2 = sem("maxed2")
        exped2 = sem("exped2")
        inv2 = sem("inv2")
        scaled2 = sem("scaled2")
        turned2 = sem("turned2")
        head_out2 = sem("head_out2")
        mix_step = sem("mix_step")
        mixed = sem("mixed")
        x_added2 = sem("x_added2")
        r_step = sem("r_step")
        r_exp = sem("r_exp")
        ranked = sem("ranked")
        turned_out = sem("turned_out")
        hrows_out = sem("hrows_out")
        slots_zero = sem("slots_zero")
        slots_clear = sem("slots_clear")
        scattered = sem("scattered")
        listed = sem("listed")
        gathered = [sem(f"gathered{n}") for n in range(2)]
        x_turned = sem("x_turned")
        silu2 = sem("silu2")
        hidden = sem("hidden")
        h_turned = sem("h_turned")
        y_evac = sem("y_evac")
        y_stored = [sem(f"y_stored{n}") for n in range(2)]
        planned = sem("planned")
        rows_ready = sem("rows_ready")
        comb_in = [sem(f"comb_in{n}") for n in range(2 * NQ)]
        comb_step = sem("comb_step")
        final_out = sem("final_out")

        block = ctx.enter_context(nc.Block())

        @block.sync
        def _(sp):
            sp.dma_start(con[:], a["con"]).then_inc(con_in, 16)
            sp.dma_start(con2[:], a["con2"]).then_inc(con_in, 16)
            sp.dma_start(pos_i[:], a["pos"].to_broadcast([P, T])).then_inc(pos_in, 16)
            sp.dma_start(posc_i[:], a["posc"]).then_inc(pos_in, 16)
            sp.dma_start(x[:], a["x"]).then_inc(x_in, 16)

            def load(l, n, src):
                if n >= RING:
                    sp.wait_ge(pe_done, done(l, *last_use(n - RING)))
                else:
                    sp.wait_ge(pe_done, done(l, *last_use(n - RING + LAYER_BLOCKS)) - PER_LAYER)
                sp.dma_start(ring[n % RING][:, 0:block_words(n)], src).then_inc(arrived[n % RING], 16)

            with sp.Fori(0, LAYERS) as l:
                sp.wait_ge(layer_end, l + 1)
                sp.dma_start(par[:], a["par"][l]).then_inc(par_in, 16)
                sp.dma_start(rel[:], a["rel"][l]).then_inc(par_in, 16)
                for n in range(FEATURE_BLOCKS):
                    load(l, n, a["w_feature"][l * FEATURE_BLOCKS + n])
                for n in range(TOKEN_BLOCKS):
                    w = block_words(FEATURE_BLOCKS + n)
                    load(l, FEATURE_BLOCKS + n, a["w_token"][l * TOKEN_BLOCKS + n, :, 0:w])
                load(l, BLOCK_MLA, a["w_uq"][l])
                load(l, BLOCK_MLA + 1, a["w_ukv"][l])
                for n in range(BLOCKS_OUT):
                    load(l, BLOCK_OUT + n, a["w_out"][l * BLOCKS_OUT + n])
                for n in range(RING):
                    load(l, BLOCK_FFN_IN + n, a["w_ffn_in"][l * JF + n])
                with sp.Fori(1, JF // RING) as r:
                    for s in range(RING):
                        sp.wait_ge(pe_done, r * (2 * RING) + (done(l, "ffn_in", s, 1) - 2 * RING))
                        slot = (BLOCK_FFN_IN + s) % RING
                        sp.dma_start(ring[slot][:], a["w_ffn_in"][l * JF + r * RING + s]).then_inc(arrived[slot], 16)
                for n in range(JF // RING * RING, JF):
                    load(l, BLOCK_FFN_IN + n, a["w_ffn_in"][l * JF + n])
                for n in range(BLOCKS_FFN_OUT):
                    load(l, BLOCK_FFN_OUT + n, a["w_ffn_out"][l * BLOCKS_FFN_OUT + n])

            def load2(n, src):
                if n >= RING:
                    sp.wait_ge(pe_done, done2(*last_use2(n - RING)))
                else:
                    sp.wait_ge(pe_done, done(LAYERS - 1, *last_use(n - RING + LAYER_BLOCKS)))
                sp.dma_start(ring[n % RING][:], src).then_inc(arrived[n % RING], 16)

            for n in range(B2_S):
                load2(n, a["w2_in"][n])
            sp.wait_ge(powers_out, 16 * ST)
            for a_ in range(YT):
                n = B2_S + 3 * a_
                if a_:
                    sp.wait_ge(cmixed, 4 * a_)
                load2(n, a["bc"][a_])
                load2(n + 1, a["w2_g"][2 * a_])
                load2(n + 2, a["w2_g"][2 * a_ + 1])
                for st in range(4 * a_, 4 * a_ + 4):
                    if st >= 2:
                        sp.wait_ge(z_ready, 2 * (st - 1))
                        sp.wait_ge(rotated, st - 1)
                    else:
                        sp.wait_ge(qk_norm, 8)
                        sp.wait_ge(cum_in, 32)
                    sp.dma_start(wtab[st % 2], powers_d[st].rearrange("p (c t) -> p c t", c=2))\
                      .then_inc(powers_in[st % 2], 16)
            sp.wait_ge(cmixed, ST)
            for n in range(B2_GLU, B2_MOE):
                load2(n, a["w2_rest"][n - B2_GLU])

            def load3(at, slot, src):
                sp.wait_ge(pe_done, at)
                sp.dma_start(ring[slot][:], src).then_inc(arrived[slot], 16)

            def expert(b):
                return sp.value_load(expert_of[0:1, bass.ds(b, 1)], min_val=0, max_val=NE - 1)

            S0 = B2_MOE % RING
            load3(done2("w_out2", KD - 5), S0, a["gate"][0])
            load3(done2("w_out2", KD - 3), (S0 + 1) % RING, a["up"][0])
            sp.wait_ge(planned, 1)
            pairs = sp.value_load(pairs_i[0:1, 0:1], min_val=0, max_val=MAX_PAIRS - NE // 2) + NE // 2
            first = sp.value_load(expert_of[0:1, 1:2], min_val=0, max_val=NE - 1)
            load3(done2("w_out2", KD - 1), (S0 + 2) % RING, a["gate"][first])
            load3(done3("gate", 0), S0, a["up"][first])
            load3(done3("up", 0), (S0 + 1) % RING, a["down"][0])
            with sp.Fori(2, pairs * 2) as b:
                e = expert(b)
                load3(done3("gate", b - 1), (S0 + 2) % RING, a["gate"][e])
                load3(done3("up", b - 1), S0, a["up"][e])
                before = expert(b - 1)
                load3(b * PER_EXPERT + (done3("down", 0, 1) - 2 * PER_EXPERT), (S0 + 1) % RING, a["down"][before])
            last = expert(pairs * 2 - 1)
            load3(done3("gate", pairs * 2 - 1), (S0 + 2) % RING, a["down"][last])
            for tc in range(NQ):
                sp.wait_ge(final_out, tc + 1)
                sp.dma_start(out[tc * P:(tc + 1) * P, :], xt[:, tc, :]).then_inc(stored, 16)
            sp.wait_ge(stored, NQ * 16)

        @block.tensor
        def _(pe):
            order = []

            def finish(ins, *name):
                order.append(name)
                return ins.then_inc(pe_done, 1)

            def weights(l, n):
                pe.wait_ge(arrived[n % RING], l * (LAYER_BLOCKS // RING * 16) + 16 * (n // RING + 1))
                return ring[n % RING]

            def norm_sum(i, dst, *name):
                for k in range(KD):
                    pe.wait_ge(squares, i * KD + (k + 1))
                    ins = pe.matmul(dst[:], c("ones"), h[:, k, :], start=k == 0, stop=k == KD - 1)
                if name:
                    finish(ins, *name)
                else:
                    ins.then_inc(pe_done, 1)

            pe.sem_inc(pe_done, PER_LAYER)
            pe.wait_ge(con_in, 32)
            with pe.Fori(0, LAYERS) as l:
                norm_sum(l * 2, bank[7], "norm", 0)
                def three(dst, high, low, at, k):
                    pe.matmul(dst, high[:, at], h_high[:, k, :], start=k == 0, stop=False)
                    pe.matmul(dst, high[:, at], h_low[:, k, :], start=False, stop=False)
                    return pe.matmul(dst, low[:, at], h_high[:, k, :], start=False, stop=k == KD - 1)

                def first_two(i, n0, slot, names, b0=0):
                    pe.wait_ge(w_split, l * SPLITS + (n0 + 1))
                    for k in range(KD):
                        pe.wait_ge(h_split, l * (3 * KD) + (i * KD + k + 1))
                        for s in range(2):
                            ins = three(bank[b0 + s][:], w_high[0], w_low[slot], slice((k * 2 + s) * P, (k * 2 + s + 1) * P), k)
                            if k == KD - 1:
                                finish(ins, *names[s])

                first_two(0, 0, 0, [("feature", 0), ("feature", 1)])
                for n in range(1, FEATURE_BLOCKS):
                    pe.wait_ge(w_split, l * SPLITS + (n + 1))
                    for s in range(2):
                        t = 2 * n + s
                        if t >= 4:
                            pe.wait_ge(feature_out, l * 14 + (t - 3))
                        for k in range(KD):
                            ins = three(bank[t % 4][:], w_high[n % 2], w_low[n % RING], slice((k * 2 + s) * P, (k * 2 + s + 1) * P), k)
                        finish(ins, "feature", t)
                pe.wait_ge(mla_squares, l * 3 + 2)
                for k in range(2):
                    ins = pe.matmul(bank[4][:], c("ones"), sq3[:, k, :], start=k == 0, stop=k == 1)
                finish(ins, "sum_q", 0)
                pe.wait_ge(mla_squares, l * 3 + 3)
                finish(pe.matmul(bank[5][:], c("ones"), sq3[:, 2, :], start=True, stop=True), "sum_kv", 0)
                for b in range(TOKEN_BLOCKS):
                    n = FEATURE_BLOCKS + b
                    pe.wait_ge(w_split, l * SPLITS + (n + 1))
                    nw = block_words(n) // KD
                    for tc in range(NQ):
                        t = b * NQ + tc
                        tok = slice(tc * P, (tc + 1) * P)
                        if t < 4:
                            pe.wait_ge(feature_out, l * 14 + min(13 + t, 14))
                        else:
                            pe.wait_ge(token_out, l * (4 * NQ) + (t - 3))
                        for k in range(KD):
                            at = slice(k * nw, (k + 1) * nw)
                            dst = bank[t % 4][:, 0:nw]
                            pe.matmul(dst, h_high[:, k, tok], w_high[n % 2][:, at], start=k == 0, stop=False)
                            pe.matmul(dst, h_low[:, k, tok], w_high[n % 2][:, at], start=False, stop=False)
                            ins = pe.matmul(dst, h_high[:, k, tok], w_low[n % RING][:, at], start=False, stop=k == KD - 1)
                        finish(ins, "token", b, tc)
                w = weights(l, BLOCK_MLA)
                pe.wait_ge(mla_normed, l * 3 + 2)
                for hd in range(MLA_H):
                    if hd < 4:
                        pe.wait_ge(token_out, l * (4 * NQ) + (8 + hd + 1))
                    else:
                        pe.wait_ge(uq_out, l * (2 * MLA_H) + (hd - 3))
                    for k in range(2):
                        ins = pe.matmul(bank[hd % 4][:], w[:, (k * MLA_H + hd) * P:(k * MLA_H + hd + 1) * P], cqkv[:, k, :],
                                        start=k == 0, stop=k == 1)
                    finish(ins, "uq", hd)
                w = weights(l, BLOCK_MLA + 1)
                pe.wait_ge(mla_normed, l * 3 + 3)
                for hd in range(MLA_H):
                    pe.wait_ge(uq_out, l * (2 * MLA_H) + (MLA_H + hd - 3))
                    finish(pe.matmul(bank[(MLA_H + hd) % 4][0:NOPE, :], w[:, hd * NOPE:(hd + 1) * NOPE], cqkv[:, 2, :],
                                     start=True, stop=True), "uk", hd)
                for tc in range(NQ):
                    pe.wait_ge(uq_out, l * (2 * MLA_H) + (2 * MLA_H + tc - 3))
                    finish(pe.matmul(bank[tc][:, 0:MLA_H * MLA_V], cqkv[:, 2, tc * P:(tc + 1) * P],
                                     w[:, MLA_H * NOPE:MLA_H * (NOPE + MLA_V)], start=True, stop=True), "uv", tc)

                for step, n in attention_order():
                    if step == "scores":
                        kind, hd, m, i = MAPS[n]
                        nk = (i + 1) * P
                        s = bank[SCORE_BANKS[n % NSB]]
                        if n >= NSB:
                            pe.wait_ge(exped, l * NMAPS + (n - NSB + 1))
                        elif n == 0:
                            pe.wait_ge(token_out, l * (4 * NQ) + 4 * NQ)
                            pe.wait_ge(uq_out, l * (2 * MLA_H) + 2 * MLA_H)
                            pe.wait_ge(roped, l * (MLA_H + 2) + (MLA_H + 2))
                        if kind == "mla":
                            kq = NOPE + ROPE
                            pe.matmul(s[:, 0:nk], qm[0:kq, hd, i * P:(i + 1) * P], km[0:kq, hd, 0:nk], start=True, stop=False)
                            ins = pe.matmul(s[:, i * P:nk], c("ident"), c("mask"), start=False, stop=True)
                        elif kind == "diff":
                            r = 2 * DIFF_QK * (hd % 2) + DIFF_QK * m
                            ins = pe.matmul(s[:, 0:nk], qk[r:r + DIFF_QK, hd // 2, i * P:(i + 1) * P],
                                            qk[r:r + DIFF_QK, 3 + hd // 2, 0:nk], start=True, stop=True)
                        else:
                            r = CH_HD * (hd % 2)
                            ins = pe.matmul(s[:, 0:nk], qk[r:r + CH_HD, 6 + hd // 2, i * P:(i + 1) * P],
                                            qk[r:r + CH_HD, 8 + hd // 2, 0:nk], start=True, stop=True)
                        finish(ins, "scores", n)
                    elif step == "turn":
                        kind, hd, i, maps = PBLOCKS[n]
                        if n >= 2:
                            pe.wait_ge(turned, l * NPB + (n - 1))
                        pe.wait_ge(scaled, l * NPB + (n + 1))
                        for kc in range(i + 1):
                            ins = pe.transpose(bank[3 + n % 2][:, kc * P:(kc + 1) * P],
                                               probs[:, maps[0] % PBUF, kc * P:(kc + 1) * P], c("ident"))
                        finish(ins, "turn", n)
                    else:
                        kind, hd, _, _ = PBLOCKS[NQ * n]
                        r = 64 * (n % 2)
                        o = bank[5 + n // 2 % 2]
                        pe.wait_ge(turned, l * NPB + NQ * (n + 1))
                        if n >= 4:
                            pe.wait_ge(head_out, l * HEADS + (n - 4 + (2 if n % 2 == 0 else 1)))
                        for kc in range(NQ):
                            if kind == "mla":
                                v = vm[:, kc, hd * MLA_V:(hd + 1) * MLA_V]
                            elif kind == "diff":
                                v = vt[:, kc, hd * DIFF_V:(hd + 1) * DIFF_V]
                            else:
                                v = vt[:, kc, (DIFF_H + hd) * DIFF_V:(DIFF_H + hd + 1) * DIFF_V]
                            ins = pe.matmul(o[r:r + 64, kc * P:T], v, pt[n % 2][:, kc, kc * P:T],
                                            start=kc == 0, stop=kc == NQ - 1)
                        finish(ins, "heads", n)

                for n, (lo, hi) in enumerate(OUT_NORM_TILES):
                    for k in range(lo, hi):
                        pe.wait_ge(out_squares, l * KD + (k + 1))
                        ins = pe.matmul(bank[n][:], c("block64") if hi == lo + 1 else c("ones"), osq[:, k, :],
                                        start=k == lo, stop=k == hi - 1)
                    finish(ins, "out_norm", n)
                first_two(1, BLOCKS_PROJ, BLOCK_OUT % RING, [("w_out", 0), ("w_out", 1)], 5)
                for b in range(1, BLOCKS_OUT):
                    pe.wait_ge(w_split, l * SPLITS + (BLOCKS_PROJ + b + 1))
                    for s in range(2):
                        m = 2 * b + s
                        pe.wait_ge(x_added, l * (2 * KD) + (m - 1))
                        for k in range(KD):
                            ins = three(bank[5 + m % 2][:], w_high[b % 2], w_low[(BLOCK_OUT + b) % RING],
                                        slice((k * 2 + s) * P, (k * 2 + s + 1) * P), k)
                        finish(ins, "w_out", m)
                norm_sum(l * 2 + 1, bank[7], "norm", 1)

                def ffn_in(slot, j, jj, used_up):
                    par_ = jj % 2
                    pe.wait_ge(w_split, j + (l * SPLITS + (SPLIT_FFN + 1)))
                    for s in range(2):
                        if used_up is not None:
                            pe.wait_ge(conv_done, used_up + s)
                        for k in range(KD):
                            ins = three(bank[2 * par_ + s][:], w_high[par_], w_low[slot], slice((k * 2 + s) * P, (k * 2 + s + 1) * P), k)
                        if isinstance(j, int):
                            finish(ins, "ffn_in", j, s)
                        else:
                            ins.then_inc(pe_done, 1)

                first_two(2, SPLIT_FFN, BLOCK_FFN_IN % RING, [("ffn_in", 0, 0), ("ffn_in", 0, 1)])
                for j in range(1, BODY):
                    ffn_in((BLOCK_FFN_IN + j) % RING, j, j, l * (2 * JF) + (2 * j - 3) if j >= 2 else None)
                with pe.Fori(1, JF // BODY) as r:
                    for s in range(BODY):
                        ffn_in((BLOCK_FFN_IN + s) % RING, r * BODY + s, s, r * (2 * BODY) + (l * (2 * JF) + (2 * s - 3)))
                for j in range(BODY, JF // BODY * BODY):
                    order.extend([("ffn_in", j, 0), ("ffn_in", j, 1)])
                for j in range(JF // BODY * BODY, JF):
                    ffn_in((BLOCK_FFN_IN + j) % RING, j, j, l * (2 * JF) + (2 * j - 3))

                for m in range(KD):
                    if m >= 2:
                        pe.wait_ge(x_added, l * (2 * KD) + (KD + m - 1))
                    for b, name in enumerate(("ffn_half", "ffn_out")):
                        pe.wait_ge(w_split, l * SPLITS + (SPLIT_OUT + 2 * m + b + 1))
                        low = w_low[(BLOCK_FFN_OUT + 2 * m + b) % RING]
                        for k in range(JF // 2):
                            kk = b * (JF // 2) + k
                            if m == 0:
                                pe.wait_ge(act_split, l * JF + (kk + 1))
                            at = slice(k * P, (k + 1) * P)
                            dst = bank[4 + m % 2][:]
                            pe.matmul(dst, w_high[b][:, at], act_high[kk], start=kk == 0, stop=False)
                            pe.matmul(dst, w_high[b][:, at], act_low[:, kk, :], start=False, stop=False)
                            ins = pe.matmul(dst, low[:, at], act_high[kk], start=False, stop=kk == JF - 1)
                        finish(ins, name, m)
            assert order == LAYER_OUT

            del order[:]
            norm_sum(2 * LAYERS, bank[7], "norm2", 0)
            norm_sum(2 * LAYERS + 1, bank[7], "norm2", 1)

            def weights2(n):
                pe.wait_ge(arrived[n % RING], RING0 + 16 * (n // RING + 1))
                return ring[n % RING]

            for t in range(YT):
                w = weights2(B2_U + t // 2)
                for k in range(KD):
                    if t == 0:
                        pe.wait_ge(normed, (2 * LAYERS + 1) * KD + k + 1)
                    ins = pe.matmul(bank[t][:], w[:, (k * 2 + t % 2) * P:(k * 2 + t % 2 + 1) * P], h[:, k, :],
                                    start=k == 0, stop=k == KD - 1)
                finish(ins, "u", t)
            for k in range(KD):
                ins = pe.matmul(bank[4][0:FH, :], con2[:, CON2["w_f"][0] + k * FH:CON2["w_f"][0] + (k + 1) * FH], h[:, k, :],
                                start=k == 0, stop=k == KD - 1)
            finish(ins, "f", 0)
            for t in range(8):
                w = weights2(B2_Q + t // 2)
                if t < 4:
                    pe.wait_ge(u_out, t + 1)
                else:
                    pe.wait_ge(qk_raw, t - 3)
                for k in range(KD):
                    ins = pe.matmul(bank[t % 4][:], w[:, (k * 2 + t % 2) * P:(k * 2 + t % 2 + 1) * P], h[:, k, :],
                                    start=k == 0, stop=k == KD - 1)
                finish(ins, "q" if t < 4 else "k", t % 4)
            for t in range(8):
                pe.wait_ge(qk_sq, t + 1)
                if t == 0:
                    pe.wait_ge(f_out, 1)
                if t >= 2:
                    pe.wait_ge(qk_log, t - 1)
                finish(pe.matmul(bank[4 + t % 2][:], c("block64"), gates[:, 8 + t, :], start=True, stop=True), "qk_sum", t)
            for b in range(2):
                w = weights2(B2_V + b)
                for tc in range(NQ):
                    if b:
                        pe.wait_ge(v_out, tc + 1)
                    elif tc == 0:
                        pe.wait_ge(qk_raw, 8)
                    for k in range(KD):
                        ins = pe.matmul(bank[tc][:, 0:256], h[:, k, tc * P:(tc + 1) * P], w[:, k * 256:(k + 1) * 256],
                                        start=k == 0, stop=k == KD - 1)
                    finish(ins, "v", b, tc)

            for st in range(ST + 1):
                if st < ST:
                    a_ = st // 4
                    w = weights2(B2_S + 3 * a_)
                    if st >= 2:
                        pe.wait_ge(z_ready, 2 * (st - 1))
                    elif st == 0:
                        pe.wait_ge(qk_log, 8)
                    for cc in range(2):
                        o = ((st % 4) * 4 + cc) * P
                        finish(pe.matmul(bank[4 + 2 * (st % 2) + cc][:], w[:, o:o + P], us[:, a_, :], start=True, stop=True),
                               "B", st, cc)
                    wg = weights2(B2_S + 3 * a_ + 1 + st % 4 // 2)
                    if st >= 2:
                        pe.wait_ge(g_out, st - 1)
                    elif st == 0:
                        pe.wait_ge(v_out, 8)
                    for k in range(KD):
                        ins = pe.matmul(bank[st % 2][:], wg[:, (k * 2 + st % 2) * P:(k * 2 + st % 2 + 1) * P], h[:, k, :],
                                        start=k == 0, stop=k == KD - 1)
                    finish(ins, "g", st)
                if st:
                    r = st - 1
                    a_ = r // 4
                    pe.wait_ge(rotated, r + 1)
                    pe.wait_ge(cmixed, r + 1)
                    if r % 4 == 0 and a_ >= 2:
                        pe.wait_ge(y_step, YSTEPS * (a_ - 2) + 1)
                    for n in range(4):
                        ins = pe.matmul(bank[2 + a_ % 2][:], cmix[r % 2][:, n if n < 2 else 2, :], cs[r % 2][:, n, :],
                                        start=r % 4 == 0 and n == 0, stop=r % 4 == 3 and n == 3)
                    finish(ins, "C", r)
            w = weights2(B2_GLU)
            for m in range(YT):
                if m == 0:
                    pe.wait_ge(gelued, YT)
                    pe.wait_ge(g_out, ST)
                for k in range(YT):
                    ins = pe.matmul(bank[m % 2][:] if m < 2 else bank[2 + m][:], w[:, (m * YT + k) * P:(m * YT + k + 1) * P],
                                    ys[:, k, :], start=k == 0, stop=k == YT - 1)
                finish(ins, "glu", m)
            for m in range(KD):
                w = weights2(B2_PSSM + m // 4)
                if m == 0:
                    pe.wait_ge(glued, YT)
                if m >= 2:
                    pe.wait_ge(ssm_mixed, m - 1)
                for k in range(YT):
                    ins = pe.matmul(bank[m % 2][:], w[:, (m % 4 * YT + k) * P:(m % 4 * YT + k + 1) * P], h[:, 4 + k, :],
                                    start=k == 0, stop=k == YT - 1)
                finish(ins, "pssm", m)
            for step, n in attention2_order():
                if step == "scores2":
                    hd, i = divmod(n, NQ)
                    nk = (i + 1) * P
                    s = bank[SCORE_BANKS[n % NSB]]
                    if n >= NSB:
                        pe.wait_ge(exped2, n - NSB + 1)
                    elif n == 0:
                        pe.wait_ge(ssm_mixed, KD)
                        pe.wait_ge(qk_norm, 16)
                        pe.wait_ge(cum_in, 32)
                    pe.matmul(s[:, 0:nk], qa[0:HROWS, hd, i * P:(i + 1) * P], ka[0:HROWS, hd, 0:nk], start=True, stop=False)
                    finish(pe.matmul(s[:, i * P:nk], c("ident"), c2("causal"), start=False, stop=True), "scores2", n)
                elif step == "turn2":
                    hd, i = divmod(n, NQ)
                    if n >= 2:
                        pe.wait_ge(turned2, n - 1)
                    pe.wait_ge(scaled2, n + 1)
                    for kc in range(i + 1):
                        ins = pe.transpose(bank[3 + n % 2][:, kc * P:(kc + 1) * P], probs2[:, n % PBUF, kc * P:(kc + 1) * P], c("ident"))
                    finish(ins, "turn2", n)
                else:
                    r = 64 * (n % 2)
                    pe.wait_ge(turned2, NQ * (n + 1))
                    if n >= 4:
                        pe.wait_ge(head_out2, n - 4 + (2 if n % 2 == 0 else 1))
                    for kc in range(NQ):
                        ins = pe.matmul(bank[5 + n // 2 % 2][r:r + 64, kc * P:T], va[:, kc, n * FD:(n + 1) * FD],
                                        ptb[n % 2][:, kc, kc * P:T], start=kc == 0, stop=kc == NQ - 1)
                    finish(ins, "heads2", n)
            for m in range(KD):
                w = weights2(B2_PATTN + m // 4)
                if m == 0:
                    pe.wait_ge(head_out2, FH)
                if m >= 2:
                    pe.wait_ge(mixed, m - 1)
                for k in range(4):
                    ins = pe.matmul(bank[m % 2][:], w[:, (m % 4 * 4 + k) * P:(m % 4 * 4 + k + 1) * P], h[:, k, :],
                                    start=k == 0, stop=k == 3)
                finish(ins, "pattn", m)
            for m in range(KD):
                w = weights2(B2_OUT + m // 2)
                if m >= 2:
                    pe.wait_ge(x_added2, m - 1)
                for k in range(KD):
                    if m == 0:
                        pe.wait_ge(mixed, k + 1)
                    ins = pe.matmul(bank[2 + m % 2][:], w[:, (k * 2 + m % 2) * P:(k * 2 + m % 2 + 1) * P], gates[:, k, :],
                                    start=k == 0, stop=k == KD - 1)
                finish(ins, "w_out2", m)
            norm_sum(2 * LAYERS + 2, bank[7], "norm2", 2)
            for k in range(KD):
                pe.wait_ge(normed, (2 * LAYERS + 2) * KD + k + 1)
                for tc in range(NQ):
                    ins = pe.matmul(bank[tc][:, 0:NR], h[:, k, tc * P:(tc + 1) * P],
                                    con2[:, CON2["w_router"][0] + k * NR:CON2["w_router"][0] + (k + 1) * NR],
                                    start=k == 0, stop=k == KD - 1)
                    if k == KD - 1:
                        finish(ins, "router", tc)
            pe.wait_ge(ranked, 1)
            for tc in range(NQ):
                for j in range(tc + 1):
                    ins = pe.matmul(bank[4][:, tc * NE:(tc + 1) * NE], c("ones") if j < tc else c2("before"), rt[:, 4, j, :],
                                    start=j == 0, stop=j == tc)
                finish(ins, "rank", tc)
            for j in range(NQ):
                ins = pe.matmul(bank[5][:, 0:NE], c("ones"), rt[:, 4, j, :], start=j == 0, stop=j == NQ - 1)
            finish(ins, "count", 0)
            for src, name, first in ((h, "ht", 0), (x, "xt", 2 * NQ)):
                for n in range(2 * NQ):
                    if first + n >= 2:
                        pe.wait_ge(turned_out, first + n - 1)
                    for k in range(4):
                        f = 4 * (n % 2) + k
                        ins = pe.transpose(bank[6 + n % 2][:, k * P:(k + 1) * P], src[:, f, n // 2 * P:(n // 2 + 1) * P], c("ident"))
                    finish(ins, name, n)
            assert order == SECOND_OUT

            S0 = B2_MOE % RING

            def have(slot, count):
                before = (B2_MOE - slot + RING - 1) // RING
                pe.wait_ge(arrived[slot], count * 16 + (RING0 + before * 16))
                return ring[slot]

            def x_turn(e, q, lacking=0):
                pe.wait_ge(gathered[q], e * 8 + (16 - 8 * q))
                for hf in range(2):
                    if not (isinstance(e, int) and e == 0):
                        pe.wait_ge(x_turned, e * 2 + (hf - 1))
                    elif hf == 0:
                        pe.wait_ge(turned_out, 4 * NQ)
                    for k in range(4):
                        ins = pe.transpose(bank[hf][:, k * P:(k + 1) * P], xg[q][:, (4 * hf + k) * P:(4 * hf + k + 1) * P], c("ident"))
                    ins.then_inc(pe_done, 1 + hf * lacking)

            def h_turn(e, q, lacking=0):
                pe.wait_ge(hidden, e + 1)
                for k in range(2):
                    ins = pe.transpose(bank[4][:, k * P:(k + 1) * P], hh[q][:, 1, k * P:(k + 1) * P], c("ident"))
                ins.then_inc(pe_done, 1 + lacking)

            def gate_up(e, q, gslot, gcount, uslot, ucount, lacking=0):
                pe.wait_ge(x_turned, e * 2 + 2)
                if not (isinstance(e, int) and e < 2):
                    pe.wait_ge(hidden, e - 1)
                for s_, (slot, count) in enumerate(((gslot, gcount), (uslot, ucount))):
                    w = have(slot, count)
                    for k in range(KD):
                        ins = pe.matmul(bank[2 + q][:, s_ * DE:(s_ + 1) * DE], xgt[q][:, k * P:(k + 1) * P],
                                        w[:, k * DE:(k + 1) * DE], start=k == 0, stop=k == KD - 1)
                    ins.then_inc(pe_done, 1 + s_ * lacking)

            def down(e, q, slot, count):
                pe.wait_ge(h_turned, e + 1)
                if not (isinstance(e, int) and e == 0):
                    pe.wait_ge(y_evac, e * 2)
                w = have(slot, count)
                for hf in range(2):
                    for k in range(2):
                        ins = pe.matmul(bank[5 + hf][:], hgt[q][:, k * P:(k + 1) * P], w[:, k * D + hf * T:k * D + (hf + 1) * T],
                                        start=k == 0, stop=k == 1)
                    ins.then_inc(pe_done, 1)

            pe.wait_ge(planned, 1)
            pairs = pe.value_load(pairs_i[0:1, 0:1], min_val=0, max_val=MAX_PAIRS - NE // 2) + NE // 2
            last = pairs * 2 - 1
            x_turn(0, 0)
            gate_up(0, 0, S0, 1, (S0 + 1) % RING, 1)
            x_turn(1, 1, lacking=2)

            def expert(e, q):
                h_turn(e - 1, 1 - q)
                gate_up(e, q, (S0 + 2) % RING, e, S0, e + 1)
                x_turn(e + 1, 1 - q)
                down(e - 1, 1 - q, (S0 + 1) % RING, e + 1)

            expert(1, 1)
            expert(2, 0)
            with pe.Fori(1, pairs - 1) as r:
                expert(r * 2 + 1, 1)
                expert(r * 2 + 2, 0)
            h_turn(last - 1, 0)
            gate_up(last, 1, (S0 + 2) % RING, last, S0, last + 1, lacking=2)
            down(last - 1, 0, (S0 + 1) % RING, last + 1)
            h_turn(last, 1, lacking=4)
            down(last, 1, (S0 + 2) % RING, last + 1)

        @block.gpsimd
        def _(pool):
            n = [0]

            def then(ins):
                n[0] += 1
                ins.then_inc(powers_step, 1)
                pool.wait_ge(powers_step, n[0])

            pool.memset(zero_i[:], 0).then_inc(slots_zero, 1)
            pool.wait_ge(slots_zero, 1)
            pool.dma_start(slots_d.rearrange("(p n) a -> p (n a)", p=P), zero_i[:]).then_inc(slots_clear, 16)
            pool.wait_ge(s5_step, S5_STEPS)
            then(pool.tensor_copy(vpow[:, 0, 0, :], s5sc[:, 1, :]))
            then(pool.tensor_copy(vpow[:, 0, 1, :], s5sc[:, 0, :]))
            for k in range(8):
                then(pool.tensor_tensor(s5t[:, 0, :], vpow[:, k, 0, :], vpow[:, k, 0, :], ALU.mult))
                then(pool.tensor_tensor(s5t[:, 1, :], vpow[:, k, 1, :], vpow[:, k, 1, :], ALU.mult))
                then(pool.tensor_tensor(vpow[:, k + 1, 0, :], s5t[:, 0, :], s5t[:, 1, :], ALU.subtract))
                then(pool.tensor_tensor(s5t[:, 0, :], vpow[:, k, 0, :], vpow[:, k, 1, :], ALU.mult))
                then(pool.tensor_tensor(vpow[:, k + 1, 1, :], s5t[:, 0, :], s5t[:, 0, :], ALU.add))
            with pool.Fori(0, ST) as st:
                def step(ins):
                    pool.drain()

                step(pool.memset(powers[0][:, 0:1], 1.0))
                step(pool.memset(powers[1][:, 0:1], 0.0))
                for k in range(9):
                    w = 2 ** k
                    vr = vpow[:, k, 0, bass.ds(st, 1)].to_broadcast([P, w])
                    vi = vpow[:, k, 1, bass.ds(st, 1)].to_broadcast([P, w])
                    re, im = powers[0][:, 0:w], powers[1][:, 0:w]
                    t0, t1 = power_tmp[0][:, 0:w], power_tmp[1][:, 0:w]
                    step(pool.tensor_tensor(t0, re, vr, ALU.mult))
                    step(pool.tensor_tensor(t1, im, vi, ALU.mult))
                    step(pool.tensor_tensor(powers[0][:, w:2 * w], t0, t1, ALU.subtract))
                    step(pool.tensor_tensor(t0, re, vi, ALU.mult))
                    step(pool.tensor_tensor(t1, im, vr, ALU.mult))
                    step(pool.tensor_tensor(powers[1][:, w:2 * w], t0, t1, ALU.add))
                pool.dma_start(powers_d[st], work[:, 41 * T:43 * T]).then_inc(powers_out, 16)
                pool.drain()

            zeros = rt[:, 0:8, :, :].rearrange("p a c e -> p (a c e)")
            pool.memset(zeros, 0.0).then_inc(slots_zero, 1)
            pool.wait_ge(slots_zero, 2)
            for b in range(NE, MAX_BLOCKS):
                pool.dma_start(yrows_d[b * P:(b + 1) * P, :], zeros).then_inc(slots_clear, 16)

            pool.wait_ge(f_step, 10)
            pool.dma_start(qa[FD:FD + 1, :, :], fg[3][0:FH, :]).then_inc(cum_in, 16)
            pool.dma_start(ka[FD + 1:FD + 2, :, :], fg[4][0:FH, :]).then_inc(cum_in, 16)
            for st in range(ST):
                pool.wait_ge(z_ready, 2 * (st + 1))
                pool.wait_ge(powers_in[st % 2], 16 * (st // 2 + 1))
                if st >= 2:
                    pool.wait_ge(pe_done, done2("C", st - 2))
                w, z, o = wtab[st % 2], zs[st % 2], cs[st % 2]
                pool.tensor_tensor(o[:, 0, :], w[:, 0, :], z[:, 0, :], ALU.mult)
                pool.tensor_tensor(o[:, 1, :], w[:, 1, :], z[:, 1, :], ALU.mult)
                pool.tensor_tensor(o[:, 2, :], w[:, 0, :], z[:, 1, :], ALU.mult)
                pool.tensor_tensor(o[:, 3, :], w[:, 1, :], z[:, 0, :], ALU.mult).then_inc(rotated, 1)

            pool.wait_ge(turned_out, 2 * NQ)
            pool.dma_start(hrows_d.rearrange("(c p) d -> p c d", p=P), ht[:]).then_inc(hrows_out, 16)
            pool.wait_ge(slots_clear, (1 + MAX_BLOCKS - NE) * 16)
            for j in range(2):
                pool.wait_ge(r_step, R_FIRST + 15 * j)
                for tc in range(NQ):
                    pool.indirect_dma_start(slots_d, bass.IndirectOffsetOnAxis(slot_i[:, 2 + j, tc:tc + 1], 0),
                                            token_i[:, tc:tc + 1], None).then_inc(scattered, 16)
            pool.wait_ge(scattered, 16 * 2 * NQ)
            pool.wait_ge(hrows_out, 16)
            pool.wait_ge(planned, 1)
            pairs = pool.value_load(pairs_i[0:1, 0:1], min_val=0, max_val=MAX_PAIRS - NE // 2) + NE // 2
            pool.dma_start(lists[:], slots_d.rearrange("(p b) a -> p (b a)", p=P)).then_inc(listed, 16)
            pool.wait_ge(listed, 16)

            def gather(e, q):
                pool.tensor_copy(list_now[q][:], lists[:, bass.ds(e, 1)])
                pool.drain()
                pool.indirect_dma_start(xg[q][:, :], None, hrows_d, bass.IndirectOffsetOnAxis(list_now[q][:, 0:1], 0))\
                    .then_inc(gathered[q], 16)

            gather(0, 0)
            gather(1, 1)

            def gather_next(e, q):
                pool.wait_ge(pe_done, done3("x_turn", e - 2, 1))
                gather(e, q)

            gather_next(2, 0)
            gather_next(3, 1)
            with pool.Fori(2, pairs) as r:
                for q in range(2):
                    gather_next(r * 2 + q, q)
            pool.wait_ge(rows_ready, 1)
            for tc in range(NQ):
                for j in range(2):
                    pool.indirect_dma_start(yg[2 * tc + j][:, :], None, yrows_d,
                                            bass.IndirectOffsetOnAxis(slot_i[:, j, tc:tc + 1], 0)).then_inc(comb_in[2 * tc + j], 16)

        @block.scalar
        def _(act):
            def root(i):
                act.activation(rstd[:, 0, :], bank[7][:], ACT.Ln, scale=1.0 / D, bias=c("eps")).then_inc(logs, 1)
                act.wait_ge(logs, i + 1)
                act.activation(rstd[:, 1, :], rstd[:, 0, :], ACT.Exp, scale=-0.5).then_inc(rstd_ready, 1)

            act.wait_ge(con_in, 32)
            act.activation(s5[:, 15, :], c2("log_dt"), ACT.Exp).then_inc(s5_act, 1)
            act.wait_ge(s5_step, 2)
            act.activation(s5r, s5a[:, 0, :], ACT.Exp).then_inc(s5_act, 1)
            act.wait_ge(s5_step, S5_ANGLE)
            act.activation(s5sc, s5ang, ACT.Sin).then_inc(s5_act, 1)
            act.wait_ge(trig_angle, 12)
            act.activation(trig[:], tmp[0][:], ACT.Sin).then_inc(trig_sin, 1)
            act.wait_ge(x_in, 16)
            act.preload_act_table_set("natural_log_exp_and_others")
            with act.Fori(0, LAYERS) as l:
                for k in range(KD):
                    if k == 0:
                        act.wait_ge(layer_end, l + 1)
                    act.activation(h[:, k, :], x[:, k, :], ACT.Square).then_inc(squares, 1)

                def split_high(n, par_, words=SLOT):
                    act.wait_ge(w_lowered, n + (l * SPLITS + 1))
                    act.activation(w_high[par_][:, 0:words], w_part[par_][:, 0:words], ACT.Copy).then_inc(w_split, 1)

                split_high(0, 0)
                act.wait_ge(pe_done, done(l, "norm", 0))
                root(l * 2)
                act.wait_ge(lam_step, l * 5 + 2)
                act.activation(lam[:, 2:4], lam[:, 0:2], ACT.Exp).then_inc(lam_exp, 1)
                split_high(1, 1)
                for k in range(KD):
                    act.wait_ge(h_lowered, l * (3 * KD) + (k + 1))
                    act.activation(h_high[:, k, :], h_part[:, k, :], ACT.Copy).then_inc(h_split, 1)
                for t in range(14):
                    act.wait_ge(pe_done, done(l, "feature", t))
                    if t < 3:
                        act.activation(cqkv[:, t, :], bank[t % 4][:], ACT.Copy).then_inc(feature_out, 1)
                    elif t == 3:
                        act.wait_ge(roped, l * (MLA_H + 2) + 1)
                        act.activation(stat[:, 0, 0:1], c("eps"), ACT.Copy).then_inc(feature_out, 1)
                        act.wait_ge(feature_out, l * 14 + 3)
                        for k in range(3):
                            act.activation(sq3[:, k, :], cqkv[:, k, :], ACT.Square).then_inc(mla_squares, 1)
                    else:
                        scale = 1.0 if 7 <= t < 10 or t >= 12 else (DIFF_SCALE if t < 7 else CH_SCALE)
                        dst = {4: 0, 5: 1, 6: 2, 7: 3, 8: 4, 9: 5, 10: 6, 11: 7, 12: 8, 13: 9}[t]
                        act.activation(qk[:, dst, :], bank[t % 4][:], ACT.Copy, scale=scale).then_inc(feature_out, 1)
                    if t % 2:
                        split_high((t + 3) // 2, (t + 3) // 2 % 2)
                act.wait_ge(pe_done, done(l, "sum_q", 0))
                act.activation(tmp[2][:], bank[4][:], ACT.Ln, scale=1.0 / Q_RANK, bias=c("eps")).then_inc(mla_logs, 1)
                act.wait_ge(pe_done, done(l, "sum_kv", 0))
                act.activation(tmp[3][:], bank[5][:], ACT.Ln, scale=1.0 / KV_RANK, bias=c("eps")).then_inc(mla_logs, 1)
                act.wait_ge(mla_logs, l * 2 + 2)
                act.activation(tmp[2][:], tmp[2][:], ACT.Exp, scale=-0.5).then_inc(mla_rstd, 1)
                act.activation(tmp[3][:], tmp[3][:], ACT.Exp, scale=-0.5).then_inc(mla_rstd, 1)
                split_high(BLOCKS_PROJ - 1, 1, block_words(BLOCKS_PROJ - 1))
                for n in range(2 * MLA_H):
                    if n < MLA_H:
                        act.wait_ge(pe_done, done(l, "uq", n))
                        act.wait_ge(roped, l * (MLA_H + 2) + (n + 3))
                        act.activation(qm[0:NOPE, n, :], bank[n % 4][0:NOPE, :], ACT.Copy, scale=MLA_SCALE).then_inc(uq_out, 1)
                    else:
                        act.wait_ge(pe_done, done(l, "uk", n - MLA_H))
                        act.activation(km[0:NOPE, n - MLA_H, :], bank[n % 4][0:NOPE, :], ACT.Copy).then_inc(uq_out, 1)

                def turn(t):
                    kind, hd, i, maps = PBLOCKS[t]
                    act.wait_ge(pe_done, done(l, "turn", t))
                    if t % NQ == 0 and t >= 2 * NQ:
                        act.wait_ge(pe_done, done(l, "heads", t // NQ - 2))
                    act.activation(pt[t // NQ % 2][:, 0:i + 1, i * P:(i + 1) * P],
                                   bank[3 + t % 2][:, 0:(i + 1) * P].rearrange("p (c q) -> p c q", q=P),
                                   ACT.Copy).then_inc(turned, 1)

                for u, (kind, hd, m, i) in enumerate(MAPS):
                    nk = (i + 1) * P
                    act.wait_ge(maxed, l * NMAPS + (u + 1))
                    src = bank[SCORE_BANKS[u % NSB]] if kind == "mla" else probs[:, u % PBUF, :]
                    if kind == "mla" and u >= PBUF:
                        act.wait_ge(pe_done, done(l, "turn", PBLOCK_OF[u - PBUF]))
                    act.activation(probs[:, u % PBUF, 0:nk], src[:, 0:nk], ACT.Exp, bias=stat[:, 0, u:u + 1],
                                   accum_out=rsum[:, u:u + 1]).then_inc(exped, 1)
                    t = PBLOCK_OF[u]
                    if u == PBLOCKS[t][3][-1] and t >= LAG:
                        turn(t - LAG)
                for t in range(NPB - LAG, NPB):
                    turn(t)
                for k in range(KD):
                    act.wait_ge(head_out, l * HEADS + 2 * (k + 1))
                    if k == 0:
                        act.wait_ge(pe_done, done(l, "heads", HEADS - 1))
                    act.activation(osq[:, k, :], h[:, k, :], ACT.Square).then_inc(out_squares, 1)
                split_high(BLOCKS_PROJ, 0)
                for n, (lo, hi) in enumerate(OUT_NORM_TILES):
                    act.wait_ge(pe_done, done(l, "out_norm", n))
                    width = 64 if hi == lo + 1 else (hi - lo) * P
                    act.activation(orst[n][:], bank[n][:], ACT.Ln, scale=1.0 / width, bias=c("eps")).then_inc(out_logs, 1)
                for n in range(5):
                    act.wait_ge(out_logs, l * 5 + (n + 1))
                    act.activation(orst[n][:], orst[n][:], ACT.Exp, scale=-0.5).then_inc(out_rstd, 1)
                split_high(BLOCKS_PROJ + 1, 1)
                for k in range(KD):
                    act.wait_ge(h_lowered, l * (3 * KD) + (KD + k + 1))
                    act.activation(h_high[:, k, :], h_part[:, k, :], ACT.Copy).then_inc(h_split, 1)
                for b in range(2, BLOCKS_OUT):
                    split_high(BLOCKS_PROJ + b, b % 2)
                act.wait_ge(pe_done, done(l, "w_out", KD - 1))
                for k in range(KD):
                    act.wait_ge(x_added, l * (2 * KD) + (k + 1))
                    act.activation(h[:, k, :], x[:, k, :], ACT.Square).then_inc(squares, 1)
                split_high(SPLIT_FFN, 0)
                act.wait_ge(pe_done, done(l, "norm", 1))
                root(l * 2 + 1)

                def conv_tap(j, par_, ready, free):
                    for s in range(2):
                        act.wait_ge(pe_done, ready + s)
                        if free is not None:
                            act.wait_ge(ffn_act, free)
                        act.activation(conv[2 * par_ + s], bank[2 * par_ + s][:], ACT.Identity,
                                       scale=conv_g(2, s, j), bias=conv_g(3, s, j)).then_inc(conv_base, 1)

                def silu(par_, ready):
                    act.wait_ge(conv_done, ready)
                    act.activation(sil[par_], conv[2 * par_ + 1], ACT.Silu).then_inc(silued, 1)

                def conv_g(tap, s, j):
                    lo = PAR["conv_w"][0] + tap * 2 * JF + s * JF
                    if isinstance(j, int):
                        return par[:, lo + j:lo + j + 1]
                    return par[:, bass.ds(j + lo, 1)]

                split_high(SPLIT_FFN + 1, 1)
                for k in range(KD):
                    act.wait_ge(h_lowered, l * (3 * KD) + (2 * KD + k + 1))
                    act.activation(h_high[:, k, :], h_part[:, k, :], ACT.Copy).then_inc(h_split, 1)
                for j in range(2):
                    conv_tap(j, j, done(l, "ffn_in", j, 0), None)
                    split_high(SPLIT_FFN + j + 2, j)
                    silu(j, l * (2 * JF) + 2 * (j + 1))
                with act.Fori(1, JF // 2 - 1) as r:
                    for s in range(2):
                        j = r * 2 + s
                        conv_tap(j, s, r * 4 + (done(l, "ffn_in", s, 0)), r * 2 + (l * JF + (s - 1)))
                        split_high(j + (SPLIT_FFN + 2), s)
                        silu(s, r * 4 + (l * (2 * JF) + 2 * (s + 1)))
                words = block_words(BLOCK_FFN_OUT)

                def act_high_parts(lo, hi):
                    for n in range(lo, hi):
                        act.wait_ge(act_lowered, l * JF + (n + 1))
                        act.activation(act_high[n], act_part[n], ACT.Copy).then_inc(act_split, 1)

                conv_tap(JF - 2, 0, done(l, "ffn_in", JF - 2, 0), l * JF + (JF - 3))
                split_high(SPLIT_OUT, 0, words)
                silu(0, l * (2 * JF) + 2 * (JF - 1))
                act_high_parts(0, EARLY)
                conv_tap(JF - 1, 1, done(l, "ffn_in", JF - 1, 0), l * JF + (JF - 2))
                split_high(SPLIT_OUT + 1, 1, words)
                act_high_parts(EARLY, EARLY + KD)
                silu(1, l * (2 * JF) + 2 * JF)
                act_high_parts(EARLY + KD, JF)
                act.preload_act_table_set("natural_log_exp_and_others")
                for n in range(2, BLOCKS_FFN_OUT):
                    split_high(SPLIT_OUT + n, n % 2, words)

            def squares_of_x():
                for k in range(KD):
                    act.activation(h[:, k, :], x[:, k, :], ACT.Square).then_inc(squares, 1)

            act.wait_ge(x_added, LAYERS * 2 * KD)
            squares_of_x()
            act.wait_ge(pe_done, done2("norm2", 0))
            root(2 * LAYERS)
            act.wait_ge(normed, (2 * LAYERS + 1) * KD)
            squares_of_x()
            act.wait_ge(pe_done, done2("norm2", 1))
            root(2 * LAYERS + 1)
            for t in range(YT):
                act.wait_ge(pe_done, done2("u", t))
                act.activation(us[:, t, :], bank[t][:], ACT.Copy).then_inc(u_out, 1)
            act.wait_ge(pe_done, done2("f", 0))
            act.activation(fg[0][0:FH, :], bank[4][0:FH, :], ACT.Identity, bias=c2("b_forget")[0:FH, :]).then_inc(f_out, 1)
            for t in range(8):
                act.wait_ge(pe_done, done2("q" if t < 4 else "k", t % 4))
                act.activation(gates[:, t, :], bank[t % 4][:], ACT.Copy).then_inc(qk_raw, 1)
                if t == 0:
                    act.wait_ge(f_step, 2)
                    act.activation(fg[2][0:FH, :], fg[1][0:FH, :], ACT.Exp, scale=-1.0).then_inc(f_step, 1)
                    act.wait_ge(f_step, 3)
                    act.activation(fg[2][0:FH, :], fg[2][0:FH, :], ACT.Ln, bias=c("ones")[0:FH, 0:1]).then_inc(f_step, 1)
                act.wait_ge(qk_raw, t + 1)
                if t == 0:
                    act.wait_ge(powers_out, 16 * ST)
                act.activation(gates[:, 8 + t, :], gates[:, t, :], ACT.Square).then_inc(qk_sq, 1)
            for t in range(8):
                act.wait_ge(pe_done, done2("qk_sum", t))
                act.activation(gates[:, 8 + t, :], bank[4 + t % 2][:], ACT.Ln, scale=1.0 / FD, bias=c("eps")).then_inc(qk_log, 1)
                act.wait_ge(qk_log, t + 1)
                act.activation(gates[:, 8 + t, :], gates[:, 8 + t, :], ACT.Exp, scale=-0.5).then_inc(qk_rst, 1)

            def gelu_sigmoid(a_):
                act.wait_ge(y_step, YSTEPS * a_ + YSTEPS)
                act.activation(y5[1][:], y5[1][:], ACT.Sigmoid, scale=2.0 * math.sqrt(2.0 / math.pi)).then_inc(y_sig, 1)

            act.wait_ge(qk_norm, 16)
            for st in range(ST):
                act.wait_ge(pe_done, done2("g", st))
                act.activation(gates[:, st, :], bank[st % 2][:], ACT.Sigmoid).then_inc(g_out, 1)
                if st >= 5 and st % 4 == 1:
                    gelu_sigmoid(st // 4 - 1)
            gelu_sigmoid(YT - 1)
            for m in range(YT):
                act.wait_ge(pe_done, done2("glu", m))
                act.activation(cs[0][:, m, :], bank[m if m < 2 else 2 + m][:], ACT.Sigmoid).then_inc(glu_sig, 1)
            act.preload_act_table_set("natural_log_exp_and_others")

            def turn2(t):
                hd, i = divmod(t, NQ)
                act.wait_ge(pe_done, done2("turn2", t))
                if i == 0 and hd >= 2:
                    act.wait_ge(pe_done, done2("heads2", hd - 2))
                if t == 0:
                    act.wait_ge(glued, YT)
                act.activation(ptb[hd % 2][:, 0:i + 1, i * P:(i + 1) * P],
                               bank[3 + t % 2][:, 0:(i + 1) * P].rearrange("p (c q) -> p c q", q=P), ACT.Copy).then_inc(turned2, 1)

            for u in range(FH * NQ):
                nk = (u % NQ + 1) * P
                act.wait_ge(maxed2, u + 1)
                if u >= PBUF:
                    act.wait_ge(pe_done, done2("turn2", u - PBUF))
                act.activation(probs2[:, u % PBUF, 0:nk], bank[SCORE_BANKS[u % NSB]][:, 0:nk], ACT.Exp, bias=stat[:, 0, u:u + 1],
                               accum_out=rsum[:, u:u + 1]).then_inc(exped2, 1)
                if u >= LAG:
                    turn2(u - LAG)
            for t in range(FH * NQ - LAG, FH * NQ):
                turn2(t)
            act.wait_ge(pe_done, done2("pattn", KD - 1))
            for k in range(KD):
                act.wait_ge(x_added2, k + 1)
                act.activation(h[:, k, :], x[:, k, :], ACT.Square).then_inc(squares, 1)
            act.wait_ge(pe_done, done2("norm2", 2))
            root(2 * LAYERS + 2)
            act.wait_ge(r_step, R_EXP)
            act.activation(rt[:, 5, :, 0:EG], rt[:, 5, :, 0:EG], ACT.Exp).then_inc(r_exp, 1)
            act.activation(rs[:, 4, :], rs[:, 3, :], ACT.Exp).then_inc(r_exp, 1)
            for n in range(4 * NQ):
                act.wait_ge(pe_done, done2("ht" if n < 2 * NQ else "xt", n % (2 * NQ)))
                dst = (ht if n < 2 * NQ else xt)
                act.activation(dst[:, n % (2 * NQ) // 2, n % 2 * T:(n % 2 + 1) * T], bank[6 + n % 2][:], ACT.Copy).then_inc(turned_out, 1)

            def act_x_turn(e, q):
                for hf in range(2):
                    act.wait_ge(pe_done, done3("x_turn", e, hf))
                    act.activation(xgt[q][:, hf * T:(hf + 1) * T], bank[hf][:], ACT.Copy).then_inc(x_turned, 1)

            def act_silu(e, q):
                act.wait_ge(pe_done, done3("up", e))
                act.activation(hh[q][:, 0, :], bank[2 + q][:, 0:DE], ACT.Silu).then_inc(silu2, 1)

            def act_store(e, q):
                act.wait_ge(y_evac, e * 2 + 2)
                act.dma_start(yrows_d.rearrange("(e p) d -> e p d", p=P)[e], yo[q][:]).then_inc(y_stored[q], 16)

            act.wait_ge(planned, 1)
            pairs = act.value_load(pairs_i[0:1, 0:1], min_val=0, max_val=MAX_PAIRS - NE // 2) + NE // 2
            last = pairs * 2 - 1
            act_x_turn(0, 0)
            act_silu(0, 0)
            act_x_turn(1, 1)
            with act.Fori(0, pairs - 1) as r:
                for q, k in ((1, 1), (0, 2)):
                    act_silu(r * 2 + k, q)
                    act_x_turn(r * 2 + (k + 1), 1 - q)
                    act_store(r * 2 + (k - 1), 1 - q)
            act_silu(last, 1)
            act_store(last - 1, 0)
            act_store(last, 1)

        @block.vector
        def _(dve):
            step = [0]

            def chain(sem_, ins, base=0):
                step[0] += 1
                ins.then_inc(sem_, 1)
                dve.wait_ge(sem_, base + step[0])

            def normalise(i, dst, gain):
                dve.wait_ge(rstd_ready, i + 1)
                for k in range(KD):
                    dve.scalar_tensor_tensor(dst[:, k, :], x[:, k, :], gain(k), rstd[:, 1, :], ALU.mult, ALU.mult)\
                       .then_inc(normed, 1)

            dve.wait_ge(pos_in, 32)
            dve.wait_ge(con_in, 32)
            TWO_PI = 2 * math.pi
            C1 = 6.28125
            C2 = 0.0019350051879882812
            C3 = TWO_PI - C1 - C2
            MAGIC = 1.5 * 2 ** 23
            made = [0]

            def s5_do(ins):
                made[0] += 1
                ins.then_inc(s5_step, 1)
                dve.wait_ge(s5_step, made[0])

            dve.wait_ge(s5_act, 1)
            th, thc = s5ang[:, 0, :], s5ang[:, 1, :]
            s5_do(dve.tensor_tensor(th, c2("a_im"), s5[:, 15, :], ALU.mult))
            s5_do(dve.tensor_tensor(s5a[:, 0, :], c2("a_re"), s5[:, 15, :], ALU.mult))
            s5_do(dve.tensor_scalar(thc, th, 1.0 / TWO_PI, MAGIC, ALU.mult, ALU.add))
            s5_do(dve.tensor_scalar(thc, thc, MAGIC, None, ALU.subtract))
            for cc in (C1, C2, C3):
                s5_do(dve.scalar_tensor_tensor(th, thc, -cc, th, ALU.mult, ALU.add))
            s5_do(dve.tensor_scalar(thc, th, math.pi / 2, None, ALU.add))
            s5_do(dve.tensor_scalar(s5den, thc, math.pi, -TWO_PI, ALU.is_gt, ALU.mult))
            s5_do(dve.tensor_tensor(thc, thc, s5den, ALU.add))
            s5_do(dve.tensor_scalar(s5ang, s5ang, 3.1415925, -3.1415925, ALU.min, ALU.max))
            assert made[0] == S5_ANGLE
            chain(trig_angle, dve.tensor_copy(tmp[1][:], pos_i[:]))
            chain(trig_angle, dve.tensor_scalar(tmp[0][:], tmp[1][:], c("inv_freq"), None, ALU.mult))
            chain(trig_angle, dve.tensor_scalar(tmp[2][:], tmp[0][:], 1.0 / TWO_PI, MAGIC, ALU.mult, ALU.add))
            chain(trig_angle, dve.tensor_scalar(tmp[2][:], tmp[2][:], MAGIC, None, ALU.subtract))
            for cc in (C1, C2, C3):
                chain(trig_angle, dve.scalar_tensor_tensor(tmp[0][:], tmp[2][:], -cc, tmp[0][:], ALU.mult, ALU.add))
            chain(trig_angle, dve.tensor_scalar(tmp[0][:], tmp[0][:], c("phase"), None, ALU.add))
            chain(trig_angle, dve.tensor_scalar(tmp[2][:], tmp[0][:], math.pi, -TWO_PI, ALU.is_gt, ALU.mult))
            chain(trig_angle, dve.tensor_tensor(tmp[0][:], tmp[0][:], tmp[2][:], ALU.add))
            chain(trig_angle, dve.tensor_scalar(tmp[0][:], tmp[0][:], 3.1415925, -3.1415925, ALU.min, ALU.max))
            chain(trig_angle, dve.tensor_copy(posc[:], posc_i[:]))
            dve.wait_ge(trig_sin, 1)
            chain(tables, dve.tensor_scalar(trig[:], trig[:], c("sign"), None, ALU.mult), -12)
            dve.memset(lam[:, 6:7], 0.0).then_inc(layer_end, 1)
            at = 0
            for i in range(NQ):
                nk = (i + 1) * P
                seg = dist[:, at:at + nk]
                chain(tables, dve.tensor_scalar(seg, tmp[1][:, 0:nk], posc[:, i:i + 1], None, ALU.subtract), -12)
                chain(tables, dve.tensor_scalar(tmp[2][:, 0:nk], seg, -1.0, None, ALU.mult), -12)
                chain(tables, dve.tensor_tensor(seg, seg, tmp[2][:, 0:nk], ALU.max), -12)
                chain(tables, dve.memset(dist[0:CHUNK, at + nk - CHUNK:at + nk], -MASKED), -12)
                at += nk

            dve.wait_ge(s5_act, 3)
            s5_do(dve.tensor_tensor(s5a[:, 0, :], s5r, s5sc[:, 1, :], ALU.mult))
            s5_do(dve.tensor_scalar(s5a[:, 0, :], s5a[:, 0, :], -1.0, None, ALU.add))
            s5_do(dve.tensor_tensor(s5a[:, 1, :], s5r, s5sc[:, 0, :], ALU.mult))
            s5_do(dve.tensor_tensor(s5b[:, 0, :], c2("a_re"), c2("a_re"), ALU.mult))
            s5_do(dve.tensor_tensor(s5b[:, 1, :], c2("a_im"), c2("a_im"), ALU.mult))
            s5_do(dve.tensor_tensor(s5den, s5b[:, 0, :], s5b[:, 1, :], ALU.add))
            s5_do(dve.reciprocal(s5den, s5den))
            s5_do(dve.tensor_tensor(s5b[:, 0, :], s5a[:, 0, :], c2("a_re"), ALU.mult))
            s5_do(dve.tensor_tensor(s5b[:, 1, :], s5a[:, 1, :], c2("a_im"), ALU.mult))
            s5_do(dve.tensor_tensor(s5cr, s5b[:, 0, :], s5b[:, 1, :], ALU.add))
            s5_do(dve.tensor_tensor(s5cr, s5cr, s5den, ALU.mult))
            s5_do(dve.tensor_tensor(s5b[:, 0, :], s5a[:, 1, :], c2("a_re"), ALU.mult))
            s5_do(dve.tensor_tensor(s5b[:, 1, :], s5a[:, 0, :], c2("a_im"), ALU.mult))
            s5_do(dve.tensor_tensor(s5ci, s5b[:, 0, :], s5b[:, 1, :], ALU.subtract))
            s5_do(dve.tensor_tensor(s5ci, s5ci, s5den, ALU.mult))
            s5_do(dve.tensor_scalar(s5nci, s5ci, -1.0, None, ALU.mult))
            assert made[0] == S5_STEPS

            with dve.Fori(0, LAYERS) as l:
                dve.wait_ge(par_in, l * 32 + 32)
                lo = PAR["lam"][0]
                lam4 = par[:, lo:lo + 4 * DIFF_QK].rearrange("p (a b d) -> p a b d", a=2, b=2)
                dve.tensor_tensor(lamp[:].rearrange("p (a d) -> p a d", a=2), lam4[:, :, 0, :], lam4[:, :, 1, :], ALU.mult)\
                   .then_inc(lam_step, 1)
                dve.wait_ge(lam_step, l * 5 + 1)
                dve.reduce_sum(lam[:, 0:2], lamp[:].rearrange("p (a d) -> p a d", a=2), AX_X).then_inc(lam_step, 1)

                def mask_and_lower(slot, par_, words, count):
                    dve.tensor_scalar(w_part[par_][:, 0:words].bitcast(I32), ring[slot][:, 0:words].bitcast(I32), HIGH_BITS,
                                      None, ALU.bitwise_and).then_inc(w_masked, 1)
                    dve.wait_ge(w_masked, count)
                    dve.tensor_tensor(w_low[slot][:, 0:words], ring[slot][:, 0:words], w_part[par_][:, 0:words],
                                      ALU.subtract).then_inc(w_lowered, 1)

                def split_proj(n):
                    if n >= 2:
                        dve.wait_ge(pe_done, done(l, *last_use(n - 2)))
                    dve.wait_ge(arrived[n % RING], l * (LAYER_BLOCKS // RING * 16) + 16 * (n // RING + 1))
                    mask_and_lower(n % RING, n % 2, block_words(n), l * SPLITS + (n + 1))

                def split_tile(i, k):
                    at = l * (3 * KD) + (i * KD + k + 1)
                    dve.tensor_scalar(h_part[:, k, :].bitcast(I32), h[:, k, :].bitcast(I32), HIGH_BITS, None, ALU.bitwise_and)\
                       .then_inc(h_masked, 1)
                    dve.wait_ge(h_masked, at)
                    dve.tensor_tensor(h_low[:, k, :], h[:, k, :], h_part[:, k, :], ALU.subtract).then_inc(h_lowered, 1)

                def normalise_and_split(norm, i, gain):
                    dve.wait_ge(rstd_ready, l * 2 + (norm + 1))
                    for k in range(KD + 1):
                        if k < KD:
                            dve.scalar_tensor_tensor(h[:, k, :], x[:, k, :], gain(k), rstd[:, 1, :], ALU.mult, ALU.mult)\
                               .then_inc(normed, 1)
                        if k:
                            dve.wait_ge(normed, l * (2 * KD) + (norm * KD + k))
                            split_tile(i, k - 1)

                split_proj(0)
                split_proj(1)
                normalise_and_split(0, 0, lambda k: g("attn_norm", k))
                dve.wait_ge(lam_exp, l + 1)
                dve.tensor_tensor(lam[:, 4:5], lam[:, 3:4], lam[:, 2:3], ALU.subtract).then_inc(lam_step, 1)
                dve.wait_ge(lam_step, l * 5 + 3)
                dve.tensor_tensor(lam[:, 5:6], lam[:, 4:5], g("lam_init", 0), ALU.subtract).then_inc(lam_step, 1)
                lo = PAR["diff_norm"][0]
                dve.tensor_scalar(gdiff[:], par[:, lo:lo + 3], g("one_minus_lam_init", 0), None, ALU.mult).then_inc(lam_step, 1)
                dve.wait_ge(lam_step, l * 5 + 5)

                def rope(src, dst, scale, n):
                    if n:
                        dve.wait_ge(roped, l * (MLA_H + 2) + (n + 1))
                    dve.scalar_tensor_tensor(rope_tmp[0][64:96, :], src[64:96, :], scale, trig[64:96, :], ALU.mult, ALU.mult)\
                       .then_inc(rope_step, 1)
                    dve.scalar_tensor_tensor(rope_tmp[1][64:96, :], src[96:128, :], scale, trig[96:128, :], ALU.mult, ALU.mult)\
                       .then_inc(rope_step, 1)
                    dve.wait_ge(rope_step, l * (2 * (MLA_H + 1)) + 2 * (n + 1))
                    return dve.tensor_tensor(dst, rope_tmp[0][64:96, :], rope_tmp[1][64:96, :], ALU.add)

                split_proj(2)
                dve.wait_ge(pe_done, done(l, "feature", 3))
                rope(bank[3], km[64:96, 0, :], 1.0, 0).then_inc(roped, 1)
                split_proj(3)
                dve.wait_ge(roped, l * (MLA_H + 2) + 1)
                dve.tensor_copy(km[64:96, 1:MLA_H, :], km[64:96, 0:1, :].to_broadcast([32, MLA_H - 1, T])).then_inc(roped, 1)
                for n in range(4, FEATURE_BLOCKS + 2):
                    split_proj(n)
                for k in range(3):
                    dve.wait_ge(mla_rstd, l * 2 + (1 if k < 2 else 2))
                    gain = g("q_norm", k) if k < 2 else g("kv_norm", 0)
                    dve.scalar_tensor_tensor(cqkv[:, k, :], cqkv[:, k, :], gain, tmp[2 if k < 2 else 3][:], ALU.mult, ALU.mult)\
                       .then_inc(mla_normed, 1)
                for b in range(TOKEN_BLOCKS):
                    nw = block_words(FEATURE_BLOCKS + b) // KD
                    for tc in range(NQ):
                        dve.wait_ge(pe_done, done(l, "token", b, tc))
                        dve.tensor_copy(vt[:, tc, b * 256:b * 256 + nw], bank[(b * NQ + tc) % 4][:, 0:nw]).then_inc(token_out, 1)
                    if b == 0:
                        split_proj(BLOCKS_PROJ - 1)
                for hd in range(MLA_H):
                    dve.wait_ge(pe_done, done(l, "uq", hd))
                    rope(bank[hd % 4], qm[64:96, hd, :], MLA_SCALE, hd + 1).then_inc(roped, 1)
                for tc in range(NQ):
                    dve.wait_ge(pe_done, done(l, "uv", tc))
                    dve.tensor_copy(vm[:, tc, :], bank[tc][:, 0:MLA_H * MLA_V]).then_inc(token_out, 1)

                def head_evac(n):
                    r = 64 * (n % 2)
                    dve.wait_ge(pe_done, done(l, "heads", n))
                    dve.tensor_copy(h[r:r + 64, n // 2, :], bank[5 + n // 2 % 2][r:r + 64, :]).then_inc(head_out, 1)

                def scale_probs(t):
                    kind, hd, i, maps = PBLOCKS[t]
                    nk = (i + 1) * P
                    u = maps[0]
                    p0 = probs[:, u % PBUF, 0:nk]
                    dve.wait_ge(exped, l * NMAPS + (maps[-1] + 1))
                    dve.reciprocal(stat[:, 1, u:maps[-1] + 1], rsum[:, u:maps[-1] + 1]).then_inc(inv_step, 1)
                    base = l * INV_TOTAL + INV_BEFORE[t]
                    dve.wait_ge(inv_step, base + 1)
                    if len(maps) == 1:
                        dve.tensor_scalar(p0, p0, stat[:, 1, u:u + 1], None, ALU.mult).then_inc(scaled, 1)
                    else:
                        p1 = probs[:, maps[1] % PBUF, 0:nk]
                        dve.tensor_scalar(p1, p1, stat[:, 1, u + 1:u + 2], lam[:, 5:6], ALU.mult, ALU.mult).then_inc(inv_step, 1)
                        dve.wait_ge(inv_step, base + 2)
                        dve.scalar_tensor_tensor(p0, p0, stat[:, 1, u:u + 1], p1, ALU.mult, ALU.add).then_inc(scaled, 1)

                for u, (kind, hd, m, i) in enumerate(MAPS):
                    nk = (i + 1) * P
                    dve.wait_ge(pe_done, done(l, "scores", u))
                    s = bank[SCORE_BANKS[u % NSB]][:, 0:nk]
                    if kind != "mla":
                        dst = probs[:, u % PBUF, 0:nk]
                        if u >= PBUF:
                            dve.wait_ge(pe_done, done(l, "turn", PBLOCK_OF[u - PBUF]))
                        if kind == "diff":
                            at = P * i * (i + 1) // 2
                            dve.scalar_tensor_tensor(dst, dist[:, at:at + nk], -SLOPES[hd], s, ALU.mult, ALU.add)\
                               .then_inc(biased, 1)
                        else:
                            dve.tensor_tensor(dst, s, rel[:, hd, T - nk:T], ALU.add).then_inc(biased, 1)
                        dve.wait_ge(biased, l * (NMAPS - MLA_H * NQ) + (u - MLA_H * NQ + 1))
                        s = dst
                    dve.tensor_reduce(stat[:, 0, u:u + 1], s, AX_X, ALU.max, negate=True).then_inc(maxed, 1)
                    t = PBLOCK_OF[u]
                    if PBLOCKS[t][3][0] == u and t >= 1:
                        scale_probs(t - 1)
                        if t > NQ + LAG and (t - 1 - NQ - LAG) % NQ == 0:
                            head_evac((t - 1 - NQ - LAG) // NQ)
                scale_probs(NPB - 1)
                for n in range((NPB - 2 - NQ - LAG) // NQ + 1, HEADS):
                    head_evac(n)

                def split_w_out(b):
                    n = BLOCK_OUT + b
                    dve.wait_ge(arrived[n % RING], l * (LAYER_BLOCKS // RING * 16) + 16 * (n // RING + 1))
                    mask_and_lower(n % RING, b % 2, SLOT, l * SPLITS + (BLOCKS_PROJ + b + 1))

                split_w_out(0)
                split_w_out(1)
                for n, (lo, hi) in enumerate(OUT_NORM_TILES):
                    dve.wait_ge(out_rstd, l * 5 + (n + 1))
                    for k in range(lo, hi):
                        gain = g("mla_out", k) if k < 3 else (gdiff[:, k - 3:k - 2] if k < 6 else g("chunk_out", k - 6))
                        dve.scalar_tensor_tensor(h[:, k, :], h[:, k, :], gain, orst[n][:], ALU.mult, ALU.mult)\
                           .then_inc(out_normed, 1)
                        if k:
                            dve.wait_ge(out_normed, l * KD + k)
                            split_tile(1, k - 1)
                dve.wait_ge(out_normed, l * KD + KD)
                split_tile(1, KD - 1)
                for m in range(KD):
                    dve.wait_ge(pe_done, done(l, "w_out", m))
                    if m % 2 and m // 2 + 2 < BLOCKS_OUT:
                        split_w_out(m // 2 + 2)
                    dve.tensor_tensor(x[:, m, :], x[:, m, :], bank[5 + m % 2][:], ALU.add).then_inc(x_added, 1)

                def split(j, jj):
                    n = BLOCK_FFN_IN + jj
                    dve.wait_ge(arrived[n % RING], l * (LAYER_BLOCKS // RING * 16)
                                + (0 if isinstance(j, int) else r * (BODY // RING * 16)) + 16 * (n // RING + 1))
                    mask_and_lower(n % RING, jj % 2, SLOT, j + (l * SPLITS + (SPLIT_FFN + 1)))

                split(0, 0)
                split(1, 1)
                normalise_and_split(1, 2, lambda k: g("ffn_norm", k))

                def conv_g(tap, s, j):
                    lo = PAR["conv_w"][0] + tap * 2 * JF + s * JF
                    return par[:, lo + j:lo + j + 1] if isinstance(j, int) else par[:, bass.ds(j + lo, 1)]

                def conv_rest(j, jj):
                    par_ = jj % 2
                    for s in range(2):
                        cv = conv[2 * par_ + s]
                        b = bank[2 * par_ + s]
                        at = j * 2 + (l * (2 * JF) + (s + 1))
                        dve.wait_ge(conv_base, at)
                        dve.scalar_tensor_tensor(cv[:, 1:T], b[:, 0:T - 1], conv_g(1, s, j), cv[:, 1:T], ALU.mult, ALU.add)\
                           .then_inc(conv_step, 1)
                        dve.wait_ge(conv_step, at)
                        dve.scalar_tensor_tensor(cv[:, 2:T], b[:, 0:T - 2], conv_g(0, s, j), cv[:, 2:T], ALU.mult, ALU.add)\
                           .then_inc(conv_done, 1)
                    dve.wait_ge(conv_done, j * 2 + (l * (2 * JF) + 2))
                    dve.wait_ge(silued, j + (l * JF + 1))
                    hidden_j = act_ff[:, j:j + 1, :] if isinstance(j, int) else act_ff[:, bass.ds(j, 1), :]
                    dve.tensor_tensor(hidden_j, sil[par_].rearrange("p (a t) -> p a t", a=1),
                                      conv[2 * par_].rearrange("p (a t) -> p a t", a=1), ALU.mult).then_inc(ffn_act, 1)

                with dve.Fori(0, JF // BODY) as r:
                    for s in range(BODY):
                        dve.wait_ge(pe_done, r * (2 * BODY) + done(l, "ffn_in", s, 1))
                        split(r * BODY + (s + 2), s + 2)
                        conv_rest(r * BODY + s, s)
                def split_out(i):
                    n = BLOCK_FFN_OUT + i
                    dve.wait_ge(arrived[n % RING], l * (LAYER_BLOCKS // RING * 16) + 16 * (n // RING + 1))
                    mask_and_lower(n % RING, i % 2, block_words(n), l * SPLITS + (SPLIT_OUT + i + 1))

                def split_act(lo, hi):
                    for n in range(lo, hi):
                        dve.wait_ge(ffn_act, l * JF + (n + 1))
                        dve.tensor_scalar(act_part[n].bitcast(I32), act_ff[:, n, :].bitcast(I32), HIGH_BITS, None, ALU.bitwise_and)\
                           .then_inc(act_masked, 1)
                        dve.wait_ge(act_masked, l * JF + (n + 1))
                        dve.tensor_tensor(act_low[:, n, :], act_ff[:, n, :], act_part[n], ALU.subtract).then_inc(act_lowered, 1)

                for j in range(JF // BODY * BODY, JF - 2):
                    dve.wait_ge(pe_done, done(l, "ffn_in", j, 1))
                    split(j + 2, j + 2)
                    conv_rest(j, j)
                dve.wait_ge(pe_done, done(l, "ffn_in", JF - 2, 1))
                split_out(0)
                conv_rest(JF - 2, JF - 2)
                split_act(0, EARLY)
                dve.wait_ge(pe_done, done(l, "ffn_in", JF - 1, 1))
                split_out(1)
                split_act(EARLY, EARLY + KD)
                conv_rest(JF - 1, JF - 1)
                split_act(EARLY + KD, JF)
                for m in range(KD):
                    if m + 1 < KD:
                        dve.wait_ge(pe_done, done(l, "ffn_half", m))
                        split_out(2 * m + 2)
                    dve.wait_ge(pe_done, done(l, "ffn_out", m))
                    if m + 1 < KD:
                        split_out(2 * m + 3)
                    ins = dve.tensor_tensor(x[:, m, :], x[:, m, :], bank[4 + m % 2][:], ALU.add).then_inc(x_added, 1)
                dve.wait_ge(x_added, l * (2 * KD) + 2 * KD)
                dve.memset(lam[:, 7:8], 0.0).then_inc(layer_end, 1)
            normalise(2 * LAYERS, x, lambda k: c("final_norm", k))
            dve.wait_ge(normed, (2 * LAYERS + 1) * KD)
            normalise(2 * LAYERS + 1, h, lambda k: c2("mix_norm", k))
            dve.wait_ge(f_out, 1)
            dve.tensor_scalar(fg[1][0:FH, :], fg[0][0:FH, :], -1.0, None, ALU.mult).then_inc(f_step, 1)
            dve.wait_ge(f_step, 1)
            dve.tensor_tensor(fg[1][0:FH, :], fg[0][0:FH, :], fg[1][0:FH, :], ALU.max).then_inc(f_step, 1)
            dve.tensor_scalar(fg[0][0:FH, :], fg[0][0:FH, :], 0.0, None, ALU.min)
            dve.wait_ge(f_step, 4)
            dve.memset(qa[64:96, :, :], 1.0).then_inc(f_step, 1)
            dve.memset(ka[64:96, :, :], 1.0).then_inc(f_step, 1)
            dve.wait_ge(f_step, 6)
            dve.tensor_tensor(fg[0][0:FH, :], fg[0][0:FH, :], fg[2][0:FH, :], ALU.subtract).then_inc(f_step, 1)
            dve.wait_ge(f_step, 7)
            dve.memset(fg[2][0:FH, :], 1.0).then_inc(f_step, 1)
            dve.wait_ge(f_step, 8)
            dve.tensor_tensor_scan(fg[3][0:FH, :], fg[2][0:FH, :], fg[0][0:FH, :], 0.0, ALU.mult, ALU.add).then_inc(f_step, 1)
            dve.wait_ge(f_step, 9)
            dve.tensor_scalar(fg[4][0:FH, :], fg[3][0:FH, :], -1.0, None, ALU.mult).then_inc(f_step, 1)
            dve.tensor_scalar(s5[:, 16, 0:1], c2("q_gain"), FD ** -0.5, None, ALU.mult).then_inc(r_step, 1)
            dve.wait_ge(r_step, 1)
            for t in range(8):
                dve.wait_ge(qk_rst, t + 1)
                dst = qa if t < 4 else ka
                gain = s5[:, 16, 0:1] if t < 4 else c2("k_gain")
                for s_ in range(2):
                    r = 64 * s_
                    dve.scalar_tensor_tensor(dst[0:FD, 2 * (t % 4) + s_, :], gates[r:r + 64, t, :], gain[r:r + 64, :],
                                             gates[r:r + 64, 8 + t, :], ALU.mult, ALU.mult).then_inc(qk_norm, 1)
            for b in range(2):
                for tc in range(NQ):
                    dve.wait_ge(pe_done, done2("v", b, tc))
                    dve.tensor_copy(va[:, tc, b * 256:(b + 1) * 256], bank[tc][:, 0:256]).then_inc(v_out, 1)

            def c_mix(st):
                w = ring[(B2_S + 3 * (st // 4)) % RING]
                o = (st % 4) * 4 * P
                cre, cim = w[:, o + 2 * P:o + 3 * P], w[:, o + 3 * P:o + 4 * P]
                cr, ci, nci = s5cr[:, st:st + 1], s5ci[:, st:st + 1], s5nci[:, st:st + 1]
                m_ = cmix[st % 2]
                dve.wait_ge(arrived[(B2_S + 3 * (st // 4)) % RING], RING0 + 16 * ((B2_S + 3 * (st // 4)) // RING + 1))
                if st >= 2:
                    dve.wait_ge(pe_done, done2("C", st - 2))
                dve.tensor_scalar(m_[:, 3, :], cim, ci, None, ALU.mult).then_inc(cmix_step, 1)
                dve.wait_ge(cmix_step, 3 * st + 1)
                dve.scalar_tensor_tensor(m_[:, 0, :], cre, cr, m_[:, 3, :], ALU.mult, ALU.subtract).then_inc(cmix_step, 1)
                dve.wait_ge(cmix_step, 3 * st + 2)
                dve.tensor_scalar(m_[:, 1, :], m_[:, 0, :], -1.0, None, ALU.mult)
                dve.tensor_scalar(m_[:, 3, :], cim, cr, None, ALU.mult).then_inc(cmix_step, 1)
                dve.wait_ge(cmix_step, 3 * st + 3)
                dve.scalar_tensor_tensor(m_[:, 2, :], cre, nci, m_[:, 3, :], ALU.mult, ALU.subtract).then_inc(cmixed, 1)

            def scan(st):
                w, z = wtab[st % 2], zs[st % 2]
                pre, pim = bank[4 + 2 * (st % 2)], bank[5 + 2 * (st % 2)]
                dve.wait_ge(powers_in[st % 2], 16 * (st // 2 + 1))
                if st >= 2:
                    dve.wait_ge(rotated, st - 1)
                dve.wait_ge(pe_done, done2("B", st, 1))
                t = cs[st % 2]
                if st >= 2:
                    dve.wait_ge(pe_done, done2("C", st - 2))
                dve.tensor_tensor(z[:, 0, :], w[:, 0, :], pre[:], ALU.mult).then_inc(z_step, 1)
                dve.tensor_tensor(t[:, 0, :], w[:, 1, :], pim[:], ALU.mult).then_inc(z_step, 1)
                dve.tensor_tensor(z[:, 1, :], w[:, 0, :], pim[:], ALU.mult).then_inc(z_step, 1)
                dve.tensor_tensor(t[:, 1, :], w[:, 1, :], pre[:], ALU.mult).then_inc(z_step, 1)
                dve.wait_ge(z_step, 6 * st + 2)
                dve.tensor_tensor(z[:, 0, :], z[:, 0, :], t[:, 0, :], ALU.add).then_inc(z_step, 1)
                dve.wait_ge(z_step, 6 * st + 4)
                dve.tensor_tensor(z[:, 1, :], z[:, 1, :], t[:, 1, :], ALU.subtract).then_inc(z_step, 1)
                decay = s5r[:, st:st + 1].to_broadcast([P, T])
                for k in range(2):
                    dve.wait_ge(z_step, 6 * st + 5 + k)
                    dve.tensor_tensor_scan(z[:, k, :], decay, z[:, k, :], 0.0, ALU.mult, ALU.add).then_inc(z_ready, 1)

            def y_do(a_, k, ins):
                ins.then_inc(y_step, 1)
                dve.wait_ge(y_step, YSTEPS * a_ + k)

            def y_poly(a_):
                dve.wait_ge(pe_done, done2("C", 4 * a_ + 3))
                y = ys[:, a_, :]
                y_do(a_, 1, dve.scalar_tensor_tensor(y, us[:, a_, :], c2("d_skip", a_), bank[2 + a_ % 2][:], ALU.mult, ALU.add))
                y_do(a_, 2, dve.tensor_tensor(y5[0][:], y, y, ALU.mult))
                if a_:
                    dve.wait_ge(gelued, a_)
                y_do(a_, 3, dve.tensor_scalar(y5[0][:], y5[0][:], 0.044715, 1.0, ALU.mult, ALU.add))
                y_do(a_, 4, dve.tensor_tensor(y5[1][:], y5[0][:], y, ALU.mult))

            def y_gelu(a_):
                dve.wait_ge(y_sig, a_ + 1)
                dve.tensor_tensor(ys[:, a_, :], ys[:, a_, :], y5[1][:], ALU.mult).then_inc(gelued, 1)

            for st in range(ST):
                c_mix(st)
                scan(st)
                if st >= 5 and st % 4 == 1:
                    y_poly(st // 4 - 1)
                if st >= 6 and st % 4 == 2:
                    y_gelu(st // 4 - 1)
            y_poly(YT - 1)
            y_gelu(YT - 1)
            for m_ in range(YT):
                dve.wait_ge(glu_sig, m_ + 1)
                dve.tensor_tensor(h[:, 4 + m_, :], ys[:, m_, :], cs[0][:, m_, :], ALU.mult).then_inc(glued, 1)
            for m_ in range(KD):
                dve.wait_ge(pe_done, done2("pssm", m_))
                dve.tensor_tensor(gates[:, KD + m_, :], gates[:, KD + m_, :], bank[m_ % 2][:], ALU.mult).then_inc(ssm_mixed, 1)

            def scale2(u):
                nk = (u % NQ + 1) * P
                dve.wait_ge(exped2, u + 1)
                dve.reciprocal(stat[:, 1, u:u + 1], rsum[:, u:u + 1]).then_inc(inv2, 1)
                dve.wait_ge(inv2, u + 1)
                p0 = probs2[:, u % PBUF, 0:nk]
                dve.tensor_scalar(p0, p0, stat[:, 1, u:u + 1], None, ALU.mult).then_inc(scaled2, 1)

            def head2(n):
                r = 64 * (n % 2)
                dve.wait_ge(pe_done, done2("heads2", n))
                dve.tensor_copy(h[r:r + 64, n // 2, :], bank[5 + n // 2 % 2][r:r + 64, :]).then_inc(head_out2, 1)

            for u in range(FH * NQ):
                nk = (u % NQ + 1) * P
                dve.wait_ge(pe_done, done2("scores2", u))
                dve.tensor_reduce(stat[:, 0, u:u + 1], bank[SCORE_BANKS[u % NSB]][:, 0:nk], AX_X, ALU.max, negate=True).then_inc(maxed2, 1)
                if u:
                    scale2(u - 1)
                if u > NQ + LAG and (u - 1 - NQ - LAG) % NQ == 0:
                    head2((u - 1 - NQ - LAG) // NQ)
            scale2(FH * NQ - 1)
            head2(FH - 1)
            for m_ in range(KD):
                dve.wait_ge(pe_done, done2("pattn", m_))
                if m_ == 0:
                    dve.wait_ge(ssm_mixed, KD)
                dve.tensor_tensor(gates[:, m_, :], gates[:, m_, :], bank[m_ % 2][:], ALU.mult).then_inc(mix_step, 1)
                dve.wait_ge(mix_step, m_ + 1)
                dve.tensor_tensor(gates[:, m_, :], gates[:, m_, :], gates[:, KD + m_, :], ALU.add).then_inc(mixed, 1)
            for m_ in range(KD):
                dve.wait_ge(pe_done, done2("w_out2", m_))
                dve.tensor_tensor(x[:, m_, :], x[:, m_, :], bank[2 + m_ % 2][:], ALU.add).then_inc(x_added2, 1)
            normalise(2 * LAYERS + 2, h, lambda k: c2("ffn_norm", k))

            made[0] = 1

            def r_do(ins):
                made[0] += 1
                ins.then_inc(r_step, 1)
                dve.wait_ge(r_step, made[0])

            def wide(v, w):
                return v.rearrange("p (c o) -> p c o", o=1).to_broadcast([P, NQ, w])

            index = c2("index")[:, 0:NE].rearrange("p (o e) -> p o e", o=1).to_broadcast([P, NQ, NE])

            def first_equal(hot, values, best, w):
                r_do(dve.tensor_tensor(hot, values, wide(best, w), ALU.is_equal))
                r_do(dve.tensor_scalar(hot, hot, -1000.0, 1000.0, ALU.mult, ALU.add))
                r_do(dve.tensor_tensor(hot, hot, index[:, :, 0:w], ALU.add))
                r_do(dve.tensor_reduce(rs[:, 23, :], hot, AX_X, ALU.min))
                r_do(dve.tensor_tensor(hot, index[:, :, 0:w], wide(rs[:, 23, :], w), ALU.is_equal))

            for tc in range(NQ):
                dve.wait_ge(pe_done, done2("router", tc))
                r_do(dve.tensor_tensor(logits[:, tc, :], bank[tc][:, 0:NR], c2("b_router"), ALU.add))
            lg = logits[:, :, 0:EG]
            dve.wait_ge(slots_clear, (1 + MAX_BLOCKS - NE) * 16)
            ge = rt[:, 5, :, 0:EG]
            r_do(dve.tensor_reduce(rs[:, 0, :], lg, AX_X, ALU.max))
            ghot = rt[:, 0, :, 0:EG]
            first_equal(ghot, lg, rs[:, 0, :], EG)
            r_do(dve.tensor_tensor(ge, lg, wide(rs[:, 0, :], EG), ALU.subtract))
            r_do(dve.tensor_scalar(ghot, ghot, BIG, -BIG, ALU.mult, ALU.add))
            le = rt[:, 1, :, :]
            for tc in range(NQ):
                r_do(dve.tensor_tensor(le[:, tc, :].rearrange("p (g e) -> p g e", g=EG),
                                       logits[:, tc, EG:NR].rearrange("p (g e) -> p g e", g=EG),
                                       ghot[:, tc, :].rearrange("p (g o) -> p g o", o=1).to_broadcast([P, EG, EPG]), ALU.add))
            hot1, hot2, le2 = rt[:, 2, :, :], rt[:, 3, :, :], rt[:, 6, :, :]
            r_do(dve.tensor_reduce(rs[:, 1, :], le, AX_X, ALU.max))
            first_equal(hot1, le, rs[:, 1, :], NE)
            r_do(dve.tensor_scalar(rt[:, 7, :, :], hot1, -3 * BIG, None, ALU.mult))
            r_do(dve.tensor_tensor(le2, le, rt[:, 7, :, :], ALU.add))
            r_do(dve.tensor_reduce(rs[:, 2, :], le2, AX_X, ALU.max))
            first_equal(hot2, le2, rs[:, 2, :], NE)
            r_do(dve.tensor_tensor(rs[:, 3, :], rs[:, 2, :], rs[:, 1, :], ALU.subtract))
            assert made[0] == R_EXP, made[0]
            dve.tensor_tensor(rt[:, 4, :, :], hot1, hot2, ALU.add).then_inc(ranked, 1)
            dve.wait_ge(r_exp, 2)
            r_do(dve.tensor_reduce(rs[:, 5, :], ge, AX_X, ALU.add))
            r_do(dve.tensor_scalar(rs[:, 6, :], rs[:, 4, :], 1.0, None, ALU.add))
            r_do(dve.tensor_tensor(rs[:, 5, :], rs[:, 5, :], rs[:, 6, :], ALU.mult))
            r_do(dve.reciprocal(rs[:, 7, :], rs[:, 5, :]))
            r_do(dve.tensor_tensor(rs[:, 8, :], rs[:, 7, :], rs[:, 4, :], ALU.mult))
            r_do(dve.tensor_copy(token_i[:], c2("token")))
            dve.wait_ge(pe_done, done2("count", 0))
            count = ends[:, 0, :]
            r_do(dve.tensor_copy(count, bank[5][:, 0:NE]))
            r_do(dve.tensor_scalar(ends[:, 1, :], count, float(P), 1.0, ALU.is_gt, ALU.add))
            for lim in (2 * P, 3 * P):
                r_do(dve.tensor_scalar(ends[:, 2, :], count, float(lim), None, ALU.is_gt))
                r_do(dve.tensor_tensor(ends[:, 1, :], ends[:, 1, :], ends[:, 2, :], ALU.add))
            r_do(dve.memset(ends[:, 2, :], 1.0))
            r_do(dve.tensor_tensor_scan(ends[:, 3, :], ends[:, 2, :], ends[:, 1, :], 0.0, ALU.mult, ALU.add))
            blocks = c2("index")
            r_do(dve.tensor_tensor(plan[:], ends[:, 3, :].rearrange("p (o e) -> p o e", o=1).to_broadcast([P, MAX_BLOCKS, NE]),
                                   blocks.rearrange("p (b o) -> p b o", o=1).to_broadcast([P, MAX_BLOCKS, NE]), ALU.is_le))
            r_do(dve.tensor_reduce(plan_f[:], plan[:], AX_X, ALU.add))
            r_do(dve.tensor_scalar(plan_f[:], plan_f[:], float(NE - 1), None, ALU.min))
            r_do(dve.tensor_copy(expert_of[:], plan_f[:]))
            r_do(dve.tensor_scalar(plan_f[:, 0:MAX_PAIRS], blocks[:, 0:MAX_PAIRS], 2.0, ends[:, 3, NE - 1:NE], ALU.mult, ALU.is_lt))
            r_do(dve.tensor_reduce(pairs_f[:, 0:1], plan_f[:, 0:MAX_PAIRS], AX_X, ALU.add))
            dve.tensor_scalar(pairs_i[:], pairs_f[:, 0:1], -float(NE // 2), None, ALU.add).then_inc(planned, 1)
            r_do(dve.tensor_tensor(ends[:, 3, :], ends[:, 3, :], ends[:, 1, :], ALU.subtract))
            first_block = ends[:, 3, :].rearrange("p (o e) -> p o e", o=1).to_broadcast([P, NQ, NE])
            dve.wait_ge(pe_done, done2("rank", NQ - 1))
            rank = rt[:, 8, :, :]
            r_do(dve.tensor_copy(rank, bank[4][:, 0:NQ * NE].rearrange("p (c e) -> p c e", c=NQ)))
            for j_, hot in enumerate((hot1, hot2)):
                o = 9 + 5 * j_
                r_do(dve.tensor_tensor(rt[:, 9, :, :], hot, rank, ALU.mult))
                r_do(dve.tensor_reduce(rs[:, o, :], rt[:, 9, :, :], AX_X, ALU.add))
                r_do(dve.tensor_tensor(rt[:, 9, :, :], hot, first_block, ALU.mult))
                r_do(dve.tensor_reduce(rs[:, o + 1, :], rt[:, 9, :, :], AX_X, ALU.add))
                r_do(dve.tensor_scalar(rs[:, o + 2, :], rs[:, o, :], float(P), None, ALU.is_ge))
                for lim in (2 * P, 3 * P):
                    r_do(dve.tensor_scalar(rs[:, o + 3, :], rs[:, o, :], float(lim), None, ALU.is_ge))
                    r_do(dve.tensor_tensor(rs[:, o + 2, :], rs[:, o + 2, :], rs[:, o + 3, :], ALU.add))
                r_do(dve.scalar_tensor_tensor(rs[:, o, :], rs[:, o + 2, :], -float(P), rs[:, o, :], ALU.mult, ALU.add))
                r_do(dve.tensor_tensor(rs[:, o + 1, :], rs[:, o + 1, :], rs[:, o + 2, :], ALU.add))
                r_do(dve.scalar_tensor_tensor(rs[:, o + 3, :], rs[:, o + 1, :], float(P), rs[:, o, :], ALU.mult, ALU.add))
                r_do(dve.tensor_copy(slot_i[:, j_, :], rs[:, o + 3, :]))
                r_do(dve.scalar_tensor_tensor(rs[:, o + 3, :], rs[:, o, :], float(MAX_BLOCKS), rs[:, o + 1, :], ALU.mult, ALU.add))
                r_do(dve.tensor_copy(slot_i[:, 2 + j_, :], rs[:, o + 3, :]))
            assert made[0] == R_STEPS, made[0]

            def dve_hidden(e, q):
                dve.wait_ge(silu2, e + 1)
                dve.wait_ge(pe_done, done3("up", e))
                dve.tensor_tensor(hh[q][:, 1, :], hh[q][:, 0, :], bank[2 + q][:, DE:2 * DE], ALU.mult).then_inc(hidden, 1)

            def dve_h_turn(e, q):
                dve.wait_ge(pe_done, done3("h_turn", e))
                dve.tensor_copy(hgt[q][:], bank[4][:, 0:2 * P]).then_inc(h_turned, 1)

            def dve_y(e, q, first=False):
                for hf in range(2):
                    dve.wait_ge(pe_done, done3("down", e, hf))
                    if not first and hf == 0:
                        dve.wait_ge(y_stored[q], e * 8 - 8 * q)
                    dve.tensor_copy(yo[q][:, hf * T:(hf + 1) * T], bank[5 + hf][:]).then_inc(y_evac, 1)

            dve.wait_ge(planned, 1)
            pairs = dve.value_load(pairs_i[0:1, 0:1], min_val=0, max_val=MAX_PAIRS - NE // 2) + NE // 2
            last = pairs * 2 - 1
            dve_hidden(0, 0)
            for e in (1, 2):
                dve_h_turn(e - 1, (e - 1) % 2)
                dve_hidden(e, e % 2)
                dve_y(e - 1, (e - 1) % 2, True)
            with dve.Fori(0, pairs - 2) as r:
                for q, k in ((1, 3), (0, 4)):
                    e = r * 2 + k
                    dve_h_turn(e - 1, 1 - q)
                    dve_hidden(e, q)
                    dve_y(e - 1, 1 - q)
            dve_h_turn(last - 1, 0)
            dve_hidden(last, 1)
            dve_y(last - 1, 0)
            dve_h_turn(last, 1)
            dve_y(last, 1)
            dve.wait_ge(y_stored[0], pairs * 16)
            dve.wait_ge(y_stored[1], pairs * 16)
            dve.memset(pairs_f[:, 1:2], 0.0).then_inc(rows_ready, 1)
            dve.wait_ge(turned_out, 4 * NQ)
            for tc in range(NQ):
                for j_ in range(2):
                    dve.wait_ge(comb_in[2 * tc + j_], 16)
                    ins = dve.scalar_tensor_tensor(xt[:, tc, :], yg[2 * tc + j_][:], rs[:, 7 + j_, tc:tc + 1], xt[:, tc, :], ALU.mult, ALU.add)
                    ins.then_inc(comb_step, 1)
                    dve.wait_ge(comb_step, 2 * tc + j_ + 1)
                dve.memset(pairs_f[:, 1:2], 0.0).then_inc(final_out, 1)


YSTEPS = 4
S5_ANGLE = 11
S5_STEPS = 27
R_EXP = 1 + 4 + 1 + 5 + 1 + 1 + 4 + 1 + 5 + 1 + 1 + 1 + 5 + 1
R_FIRST = R_EXP + 5 + 1 + 15 + 1 + 15
R_STEPS = R_FIRST + 15


INV_BEFORE = [0]
for _b in PBLOCKS:
    INV_BEFORE.append(INV_BEFORE[-1] + len(_b[3]))
INV_TOTAL = INV_BEFORE[-1]


def layout(inputs):
    import numpy as np

    f = np.float32

    def arr(name):
        return np.asarray(inputs[name])

    def tiles(w, cols):
        k = w.shape[0] // P
        return w.reshape(k, P, cols).transpose(1, 0, 2).reshape(P, k * cols)

    def columns(v):
        return v.reshape(-1, P).T

    L = LAYERS
    a = {}
    a["x"] = arr("x")[0].T.reshape(KD, P, T).transpose(1, 0, 2)
    pos = arr("positions")
    a["pos"] = pos.reshape(1, T)
    a["posc"] = columns(pos[0])
    con = np.zeros((P, CON_W), f)

    def put(name, v):
        con[:, CON[name][0]:CON[name][1]] = v

    put("ident", np.eye(P, dtype=f))
    put("ones", 1)
    put("block64", np.kron(np.eye(2, dtype=f), np.ones((64, 64), f)))
    half = ROPE // 2
    inv = (f(10000.0) ** (-np.arange(half, dtype=f) / f(half))).astype(f)
    put("inv_freq", np.tile(inv, P // half)[:, None])
    phase = np.zeros((P, 1), f)
    phase[64:96] = math.pi / 2
    put("phase", phase)
    sign = np.ones((P, 1), f)
    sign[96:96 + half] = -1
    put("sign", sign)
    put("eps", EPS)
    mask = np.zeros((P, P), f)
    mask[:CHUNK, CHUNK:] = MASKED
    put("mask", mask)
    put("final_norm", columns(arr("final_norm")))
    a["con"] = con

    par = np.zeros((L, P, PAR_W), f)

    def putl(name, v):
        par[:, :, PAR[name][0]:PAR[name][1]] = v

    for name, src in (("attn_norm", "attn_norm"), ("ffn_norm", "ffn_norm"), ("q_norm", "mla_q_norm"), ("kv_norm", "mla_kv_norm"),
                      ("mla_out", "mla_out_norm"), ("diff_norm", "diff_norm"), ("chunk_out", "chunk_out_norm"),
                      ("conv_b", "ffn_conv_b")):
        putl(name, np.stack([columns(v) for v in arr(src)]))
    putl("conv_w", np.stack([np.concatenate([columns(v) for v in w], 1) for w in arr("ffn_conv_w")]))
    putl("lam", arr("diff_lambda").reshape(L, 1, 4 * DIFF_QK))
    init = np.array([0.8 - 0.6 * math.exp(-0.3 * l) for l in range(L)])
    putl("lam_init", init.reshape(L, 1, 1))
    putl("one_minus_lam_init", (1.0 - init).reshape(L, 1, 1))
    a["par"] = par

    d = 384 + np.arange(P)[:, None] - np.arange(T)[None, :]
    rel = arr("chunk_rel_bias")[:, :, np.clip(d, -(CHUNK - 1), REL_MAX) + CHUNK - 1]
    rel[:, :, :CHUNK, T - CHUNK:] = MASKED
    a["rel"] = rel.transpose(0, 2, 1, 3)

    w_in = arr("w_in")
    kr = Q_RANK + KV_RANK
    df = kr + ROPE
    ch = df + DIFF_H * (4 * DIFF_QK + DIFF_V)
    dqk, cw = DIFF_H * 2 * DIFF_QK, CH_H * CH_HD
    swapped = np.r_[kr + half:kr + ROPE, kr:kr + half]
    feature = np.r_[0:kr, kr - 64:kr + ROPE, swapped, df:df + 2 * dqk, ch:ch + 2 * cw]
    token = np.r_[df + 2 * dqk:ch, ch + 2 * cw:ch + 3 * cw]
    a["w_feature"] = np.stack([tiles(w_in[l][:, feature[256 * n:256 * n + 256]], 256) for l in range(L) for n in range(FEATURE_BLOCKS)])
    w_token = np.zeros((L * TOKEN_BLOCKS, P, SLOT), f)
    for l in range(L):
        for n in range(TOKEN_BLOCKS):
            cols = token[256 * n:256 * n + 256]
            w_token[l * TOKEN_BLOCKS + n, :, 0:KD * len(cols)] = tiles(w_in[l][:, cols], len(cols))
    a["w_token"] = w_token
    uq = arr("mla_w_uq").reshape(L, Q_RANK, MLA_H, NOPE + ROPE)
    uq = uq[..., np.r_[0:NOPE + ROPE, NOPE + half:NOPE + ROPE, NOPE:NOPE + half]].reshape(L, Q_RANK, MLA_H * P)
    a["w_uq"] = np.stack([tiles(w, MLA_H * P) for w in uq])
    ukv = arr("mla_w_ukv").reshape(L, KV_RANK, MLA_H, 2, 64).transpose(0, 1, 3, 2, 4)
    a["w_ukv"] = ukv.reshape(L, KV_RANK, 2 * MLA_H * 64)
    a["w_out"] = np.stack([tiles(w[:, 256 * n:256 * n + 256], 256) for w in arr("w_out") for n in range(BLOCKS_OUT)])
    a["w_ffn_in"] = np.stack([tiles(w[:, np.r_[P * j:P * j + P, D_FF + P * j:D_FF + P * j + P]], 256)
                              for w in arr("w_ffn_in") for j in range(JF)])
    hb = D_FF // 2
    a["w_ffn_out"] = np.stack([tiles(w[hb * b:hb * b + hb, P * m:P * m + P], P)
                               for w in arr("w_ffn_out") for m in range(KD) for b in range(2)])

    def two(name):
        return arr(name + "_2")[0]

    con2 = np.zeros((P, CON2_W), f)

    def put2(name, v):
        con2[:, CON2[name][0]:CON2[name][1]] = v

    put2("mix_norm", columns(two("norm_mix_g")))
    put2("ffn_norm", columns(two("norm_ffn_g")))
    put2("q_gain", np.tile(two("q_norm_g"), 2)[:, None])
    put2("k_gain", np.tile(two("k_norm_g"), 2)[:, None])
    con2[:FH, CON2["b_forget"][0]] = two("b_forget")
    put2("d_skip", columns(two("ssm_D")))
    put2("a_re", columns(two("ssm_A_re").reshape(-1)))
    put2("a_im", columns(two("ssm_A_im").reshape(-1)))
    put2("log_dt", columns(np.repeat(two("ssm_log_dt"), SN)))
    w2 = two("w_in")
    fcol = 3 * FH * FD
    put2("w_f", tiles(w2[:, fcol:fcol + FH], FH))
    put2("w_router", tiles(np.concatenate([two("w_router_group"), two("w_router_expert")], 1), NR))
    put2("b_router", np.concatenate([two("b_router_group"), two("b_router_expert")])[None, :])
    i = np.arange(P)
    put2("causal", np.where(i[None, :] > i[:, None], f(-1e30), f(0)))
    put2("before", (i[:, None] < i[None, :]).astype(f))
    put2("token", i[:, None] + P * np.arange(NQ)[None, :])
    put2("index", np.arange(MAX_BLOCKS)[None, :])
    a["con2"] = con2
    ucol = fcol + FH
    order = np.r_[ucol:ucol + SSM, 0:fcol]
    a["w2_in"] = np.stack([tiles(w2[:, order[256 * n:256 * n + 256]], 256) for n in range(B2_S)])
    gcol = ucol + SSM
    a["w2_g"] = np.stack([tiles(w2[:, gcol + 256 * n:gcol + 256 * n + 256], 256) for n in range(2 * YT)])
    bc = np.zeros((YT, P, 4, 4, P), f)
    for gi in range(SG):
        st, half_ = divmod(gi, 2)
        ch0, n0 = gi % 8 * SC, half_ * SN
        for k, name in enumerate(("ssm_B_re", "ssm_B_im")):
            bc[st // 4, ch0:ch0 + SC, st % 4, k, n0:n0 + SN] = two(name)[gi].T
        for k, name in enumerate(("ssm_C_re", "ssm_C_im")):
            bc[st // 4, n0:n0 + SN, st % 4, 2 + k, ch0:ch0 + SC] = two(name)[gi].T
    a["bc"] = bc.reshape(YT, P, SLOT)

    def square(w, n_out):
        k = w.shape[0] // P
        t = w.reshape(k, P, -1, P).transpose(2, 1, 0, 3)
        t = t.reshape(-1, n_out, P, k, P).transpose(0, 2, 1, 3, 4)
        return list(t.reshape(t.shape[0], P, -1))

    wo = two("w_out")
    rest = square(two("w_glu"), YT) + square(two("w_proj_ssm"), 4) + square(two("w_proj_attn"), 4)
    rest += [tiles(wo[:, 256 * n:256 * n + 256], 256) for n in range(4)]
    a["w2_rest"] = np.stack(rest)
    for name, src in (("gate", "w_expert_gate"), ("up", "w_expert_up")):
        a[name] = two(src).reshape(NE, KD, P, DE).transpose(0, 2, 1, 3).reshape(NE, P, KD * DE)
    a["down"] = two("w_expert_down").reshape(NE, 2, P, D).transpose(0, 2, 1, 3).reshape(NE, P, 2 * D)
    return {f"in_{k}": np.ascontiguousarray(v) for k, v in a.items()}


def kernel(**inputs):
    import numpy as np
    import concourse.bacc as bacc
    from concourse import mybir as mb
    from concourse.bass_utils import run_bass_kernel_spmd as run

    nc = bacc.Bacc("TRN2", target_bir_lowering=False, num_devices=1)
    arrays = layout(inputs)
    args = {k[3:]: nc.dram_tensor(k, v.shape, mb.dt.from_np(v.dtype), kind="ExternalInput").ap() for k, v in arrays.items()}
    out = nc.dram_tensor("out", (T, D), F32, kind="ExternalOutput").ap()
    build(nc, args, out)
    r = run(nc, [arrays], core_ids=[0])
    return r.results[0]["out"].reshape(1, T, D)
```
